# Optimizing a Trainium2 kernel written in Bass

```python
import math
import jax
import jax.numpy as jnp
from jax import lax
import numpy as np

D_MODEL = 1024
BATCH = 1
SEQ = 512
DEPTH = 1
DEC_BATCH = 8
DEC_SEQ = 8
PAST_LEN = 2048
PAGE_SIZE = 128

NORM_EPS = 1e-6
SSM_D_INNER = 2 * D_MODEL
SSM_HEAD_DIM = 64
SSM_N_HEADS = SSM_D_INNER // SSM_HEAD_DIM
SSM_N_GROUPS = 8
SSM_D_STATE = 128
SSM_CONV_WIDTH = 4
SSM_CONV_DIM = SSM_D_INNER + 2 * SSM_N_GROUPS * SSM_D_STATE
SSM_BC_WIDTH = SSM_N_GROUPS * SSM_D_STATE
SSM_CHUNK = 128
ATTN_HEAD_DIM = 64
ATTN_N_HEADS = D_MODEL // ATTN_HEAD_DIM
ATTN_N_KV_HEADS = 4
ATTN_Q_PER_KV = ATTN_N_HEADS // ATTN_N_KV_HEADS
ATTN_Q_WIDTH = ATTN_N_HEADS * ATTN_HEAD_DIM
ATTN_KV_WIDTH = ATTN_N_KV_HEADS * ATTN_HEAD_DIM
WINDOW = 128
ROPE_THETA = 10000.0
PEER_N_KEYS = 128
PEER_N_EXPERTS = PEER_N_KEYS * PEER_N_KEYS
PEER_HEADS = 8
PEER_QUERY_DIM = 128
PEER_HALF_DIM = PEER_QUERY_DIM // 2
PEER_TOPK = 16
PEER_BLOCK = 128
IN_SPLIT_SIZES = (SSM_D_INNER, SSM_CONV_DIM, SSM_N_HEADS, ATTN_Q_WIDTH, ATTN_KV_WIDTH, ATTN_KV_WIDTH, D_MODEL, D_MODEL)
IN_WIDTH = SSM_D_INNER + SSM_CONV_DIM + SSM_N_HEADS + ATTN_Q_WIDTH + 2 * ATTN_KV_WIDTH + 2 * D_MODEL

kernel_name = 'hybrid_ssd_swa_sink_peer_step'

def rms_norm(x, w):
    xf = x.astype(jnp.float32)
    y = xf * lax.rsqrt(jnp.mean(xf * xf, axis=-1, keepdims=True) + NORM_EPS)
    return (y * w.astype(jnp.float32)).astype(x.dtype)

def split_in_proj(proj):
    offsets = []
    acc = 0
    for size in IN_SPLIT_SIZES[:-1]:
        acc += size
        offsets.append(acc)
    return jnp.split(proj, offsets, axis=-1)

def rope(x, pos):
    half = x.shape[-1] // 2
    inv = ROPE_THETA ** (-jnp.arange(half, dtype=jnp.float32) / half)
    ang = pos.astype(jnp.float32)[:, None] * inv[None, :]
    cos = jnp.cos(ang)[None, :, None, :]
    sin = jnp.sin(ang)[None, :, None, :]
    xf = x.astype(jnp.float32)
    x1, x2 = xf[..., :half], xf[..., half:]
    return jnp.concatenate([x1 * cos - x2 * sin, x2 * cos + x1 * sin], axis=-1).astype(x.dtype)

def causal_dwconv(u, prev, w, b):
    c = u.shape[-1]
    up = jnp.concatenate([prev.astype(u.dtype), u], axis=1)
    y = lax.conv_general_dilated(up, w.astype(u.dtype)[:, None, :], window_strides=(1,), padding='VALID',
                                 dimension_numbers=('NWC', 'WIO', 'NWC'), feature_group_count=c)
    return y + b.astype(u.dtype), up[:, -(SSM_CONV_WIDTH - 1):]

def ssd_scan(x, dt, a, bmat, cmat, init_state, chunk):
    bsz, l, nh, hp = x.shape
    g, n = bmat.shape[2], bmat.shape[3]
    r = nh // g
    c = l // chunk
    f32 = jnp.float32
    xdt = (x.astype(f32) * dt[..., None]).reshape(bsz, c, chunk, g, r, hp)
    a_cum = jnp.cumsum((dt * a).reshape(bsz, c, chunk, g, r), axis=2)
    bc = bmat.astype(f32).reshape(bsz, c, chunk, g, n)
    cc = cmat.astype(f32).reshape(bsz, c, chunk, g, n)
    causal = jnp.tril(jnp.ones((chunk, chunk), dtype=bool))[:, :, None, None]
    seg = a_cum[:, :, :, None] - a_cum[:, :, None, :]
    decay = jnp.exp(jnp.where(causal, seg, -jnp.inf))
    cb = jnp.einsum('bctgn,bcsgn->bctsg', cc, bc)
    y_diag = jnp.einsum('bctsg,bctsgr,bcsgrp->bctgrp', cb, decay, xdt)
    decay_to_end = jnp.exp(a_cum[:, :, -1:] - a_cum)
    chunk_states = jnp.einsum('bctgn,bctgr,bctgrp->bcgrpn', bc, decay_to_end, xdt)
    chunk_decay = jnp.exp(a_cum[:, :, -1])

    def step(s, inp):
        cs, cd = inp
        return s * cd[..., None, None] + cs, s

    final, prev = lax.scan(step, init_state.reshape(bsz, g, r, hp, n),
                           (jnp.moveaxis(chunk_states, 1, 0), jnp.moveaxis(chunk_decay, 1, 0)))
    prev = jnp.moveaxis(prev, 0, 1)
    y_off = jnp.einsum('bctgn,bcgrpn,bctgr->bctgrp', cc, prev, jnp.exp(a_cum))
    y = (y_diag + y_off).reshape(bsz, l, nh, hp)
    return y, final.reshape(bsz, nh, hp, n)

def mamba_branch(z, xbc, dt_raw, conv_prev, ssm_prev, lw):
    bsz, l, _ = xbc.shape
    f32 = jnp.float32
    u, conv_new = causal_dwconv(xbc, conv_prev, lw['conv_w'], lw['conv_b'])
    u = jax.nn.silu(u)
    xs = u[..., :SSM_D_INNER].reshape(bsz, l, SSM_N_HEADS, SSM_HEAD_DIM)
    bm = u[..., SSM_D_INNER:SSM_D_INNER + SSM_BC_WIDTH].reshape(bsz, l, SSM_N_GROUPS, SSM_D_STATE)
    cm = u[..., SSM_D_INNER + SSM_BC_WIDTH:].reshape(bsz, l, SSM_N_GROUPS, SSM_D_STATE)
    dt = jax.nn.softplus(dt_raw.astype(f32) + lw['dt_bias'].astype(f32))
    a = -jnp.exp(lw['a_log'].astype(f32))
    chunk = SSM_CHUNK if l % SSM_CHUNK == 0 else l
    y, ssm_new = ssd_scan(xs, dt, a, bm, cm, ssm_prev.astype(f32), chunk)
    y = y + xs.astype(f32) * lw['d_skip'].astype(f32)[:, None]
    y = y.reshape(bsz, l, SSM_D_INNER) * jax.nn.silu(z.astype(f32))
    yg = y.reshape(bsz, l, SSM_N_GROUPS, SSM_D_INNER // SSM_N_GROUPS)
    yg = yg * lax.rsqrt(jnp.mean(yg * yg, axis=-1, keepdims=True) + NORM_EPS)
    y = (yg.reshape(bsz, l, SSM_D_INNER) * lw['ssm_norm_w'].astype(f32)).astype(z.dtype)
    return y @ lw['w_ssm_out'], conv_new, ssm_new.astype(ssm_prev.dtype)

def sink_softmax(s, sink):
    m = jnp.maximum(jnp.max(s, axis=-1, keepdims=True), sink)
    p = jnp.exp(s - m)
    return p / (jnp.sum(p, axis=-1, keepdims=True) + jnp.exp(sink - m))

def swa_prompt(q, k, v, sinks):
    bsz, l, _, d = q.shape
    nb = l // WINDOW
    f32 = jnp.float32
    qb = q.astype(f32).reshape(bsz, nb, WINDOW, ATTN_N_KV_HEADS, ATTN_Q_PER_KV, d)
    kb = k.astype(f32).reshape(bsz, nb, WINDOW, ATTN_N_KV_HEADS, d)
    vb = v.astype(f32).reshape(bsz, nb, WINDOW, ATTN_N_KV_HEADS, d)
    shift = lambda t: jnp.concatenate([jnp.zeros_like(t[:, :1]), t[:, :-1]], axis=1)
    kk = jnp.concatenate([shift(kb), kb], axis=2)
    vv = jnp.concatenate([shift(vb), vb], axis=2)
    qi = jnp.arange(WINDOW)[:, None]
    ki = jnp.arange(2 * WINDOW)[None, :] - WINDOW
    band = (ki <= qi) & (qi - ki < WINDOW)
    valid = band[None] & ((jnp.arange(nb)[:, None, None] > 0) | (ki[None] >= 0))
    s = jnp.einsum('bnqhrd,bnkhd->bnhrqk', qb, kk) * (d ** -0.5)
    s = jnp.where(valid[None, :, None, None], s, -jnp.inf)
    p = sink_softmax(s, sinks.astype(f32).reshape(1, 1, ATTN_N_KV_HEADS, ATTN_Q_PER_KV, 1, 1))
    o = jnp.einsum('bnhrqk,bnkhd->bnqhrd', p, vv)
    return o.reshape(bsz, l, ATTN_Q_WIDTH).astype(q.dtype)

def swa_sample(q, k, v, k_buf, v_buf, sinks, pos0):
    bsz, l, _, d = q.shape
    wb = k_buf.shape[1]
    f32 = jnp.float32
    kk = jnp.concatenate([k_buf, k.astype(k_buf.dtype)], axis=1)
    vv = jnp.concatenate([v_buf, v.astype(v_buf.dtype)], axis=1)
    qpos = pos0 + jnp.arange(l)
    kpos = pos0 - wb + jnp.arange(wb + l)
    valid = (kpos[None, :] <= qpos[:, None]) & (qpos[:, None] - kpos[None, :] < WINDOW)
    qg = q.astype(f32).reshape(bsz, l, ATTN_N_KV_HEADS, ATTN_Q_PER_KV, d)
    s = jnp.einsum('bqhrd,bkhd->bhrqk', qg, kk.astype(f32)) * (d ** -0.5)
    s = jnp.where(valid, s, -jnp.inf)
    p = sink_softmax(s, sinks.astype(f32).reshape(1, ATTN_N_KV_HEADS, ATTN_Q_PER_KV, 1, 1))
    o = jnp.einsum('bhrqk,bkhd->bqhrd', p, vv.astype(f32))
    return o.reshape(bsz, l, ATTN_Q_WIDTH).astype(q.dtype), kk[:, -wb:], vv[:, -wb:]

def peer_ffn(h, w_q, sub_keys, u_tab, v_tab):
    shape = h.shape
    f32 = jnp.float32
    hf = h.reshape(-1, D_MODEL)
    t = hf.shape[0]
    q = (hf @ w_q).astype(f32).reshape(t, PEER_HEADS, 2, PEER_HALF_DIM)
    s = jnp.einsum('thjd,jnd->thjn', q, sub_keys.astype(f32))
    sv, si = lax.top_k(s, PEER_TOPK)
    comb = (sv[:, :, 0, :, None] + sv[:, :, 1, None, :]).reshape(t, PEER_HEADS, PEER_TOPK * PEER_TOPK)
    cand = (si[:, :, 0, :, None] * PEER_N_KEYS + si[:, :, 1, None, :]).reshape(t, PEER_HEADS, PEER_TOPK * PEER_TOPK)
    best, pick = lax.top_k(comb, PEER_TOPK)
    experts = jnp.take_along_axis(cand, pick, axis=-1)
    gates = jax.nn.softmax(best, axis=-1)
    pad = (-t) % PEER_BLOCK
    nb = (t + pad) // PEER_BLOCK
    hp = jnp.pad(hf, ((0, pad), (0, 0))).reshape(nb, PEER_BLOCK, D_MODEL)
    ep = jnp.pad(experts, ((0, pad), (0, 0), (0, 0))).reshape(nb, PEER_BLOCK, PEER_HEADS, PEER_TOPK)
    gp = jnp.pad(gates, ((0, pad), (0, 0), (0, 0))).reshape(nb, PEER_BLOCK, PEER_HEADS, PEER_TOPK)

    def expert_block(args):
        hb, eb, gb = args
        act = jax.nn.gelu(jnp.einsum('td,thkd->thk', hb, u_tab[eb]).astype(f32), approximate=False)
        return jnp.einsum('thk,thkd->td', (gb * act).astype(hb.dtype), v_tab[eb])

    out = lax.map(expert_block, (hp, ep, gp))
    return out.reshape(-1, D_MODEL)[:t].reshape(shape)

def trunk_layer(x, conv_prev, ssm_prev, k_buf, v_buf, pos0, lw):
    bsz, l, _ = x.shape
    h = rms_norm(x, lw['norm_mix_w'])
    z, xbc, dt_raw, q, k, v, gate_ssm, gate_attn = split_in_proj(h @ lw['w_in'])
    y_ssm, conv_new, ssm_new = mamba_branch(z, xbc, dt_raw, conv_prev, ssm_prev, lw)
    pos = pos0 + jnp.arange(l)
    q = rope(q.reshape(bsz, l, ATTN_N_HEADS, ATTN_HEAD_DIM), pos)
    k = rope(k.reshape(bsz, l, ATTN_N_KV_HEADS, ATTN_HEAD_DIM), pos)
    v = v.reshape(bsz, l, ATTN_N_KV_HEADS, ATTN_HEAD_DIM)
    if k_buf is None:
        o = swa_prompt(q, k, v, lw['attn_sinks'])
        keep = min(WINDOW, l)
        k_new, v_new = k[:, l - keep:], v[:, l - keep:]
    else:
        o, k_new, v_new = swa_sample(q, k, v, k_buf, v_buf, lw['attn_sinks'], pos0)
    y_attn = o @ lw['w_attn_out']
    merged = jax.nn.sigmoid(gate_ssm) * y_ssm + jax.nn.sigmoid(gate_attn) * y_attn
    x = x + merged @ lw['w_out']
    x = x + peer_ffn(rms_norm(x, lw['norm_ffn_w']), lw['peer_w_q'], lw['peer_sub_keys'], lw['peer_u'], lw['peer_v'])
    return x, conv_new, ssm_new, k_new, v_new

def setup_inputs(seed: int = 0) -> dict:
    key = jax.random.key(seed)
    ks = list(jax.random.split(key, 32))
    nrm = lambda i, shape, scale: scale * jax.random.normal(ks[i], shape, jnp.float32)
    wb = min(WINDOW, PAST_LEN)
    dt0 = jnp.exp(jax.random.uniform(ks[10], (DEPTH, SSM_N_HEADS), jnp.float32, math.log(1e-3), math.log(1e-1)))
    return {
        'x_prompt': nrm(0, (BATCH, SEQ, D_MODEL), 1.0),
        'x_sample': nrm(1, (DEC_BATCH, DEC_SEQ, D_MODEL), 1.0),
        'state_conv': nrm(2, (DEPTH, DEC_BATCH, SSM_CONV_WIDTH - 1, SSM_CONV_DIM), 1.0),
        'state_ssm': nrm(3, (DEPTH, DEC_BATCH, SSM_N_HEADS, SSM_HEAD_DIM, SSM_D_STATE), 0.1),
        'cache_k_window': nrm(4, (DEPTH, DEC_BATCH, wb, ATTN_N_KV_HEADS, ATTN_HEAD_DIM), 1.0),
        'cache_v_window': nrm(5, (DEPTH, DEC_BATCH, wb, ATTN_N_KV_HEADS, ATTN_HEAD_DIM), 1.0),
        'norm_mix_w': 1.0 + nrm(6, (DEPTH, D_MODEL), 0.05),
        'w_in': nrm(7, (DEPTH, D_MODEL, IN_WIDTH), D_MODEL ** -0.5),
        'conv_w': nrm(8, (DEPTH, SSM_CONV_WIDTH, SSM_CONV_DIM), SSM_CONV_WIDTH ** -0.5),
        'conv_b': nrm(9, (DEPTH, SSM_CONV_DIM), 0.01),
        'dt_bias': dt0 + jnp.log(-jnp.expm1(-dt0)),
        'a_log': jnp.log(jax.random.uniform(ks[11], (DEPTH, SSM_N_HEADS), jnp.float32, 1.0, 16.0)),
        'd_skip': 1.0 + nrm(12, (DEPTH, SSM_N_HEADS), 0.1),
        'ssm_norm_w': 1.0 + nrm(13, (DEPTH, SSM_D_INNER), 0.05),
        'w_ssm_out': nrm(14, (DEPTH, SSM_D_INNER, D_MODEL), SSM_D_INNER ** -0.5),
        'attn_sinks': nrm(15, (DEPTH, ATTN_N_HEADS), 0.5),
        'w_attn_out': nrm(16, (DEPTH, ATTN_Q_WIDTH, D_MODEL), ATTN_Q_WIDTH ** -0.5),
        'w_out': nrm(17, (DEPTH, D_MODEL, D_MODEL), D_MODEL ** -0.5),
        'norm_ffn_w': 1.0 + nrm(18, (DEPTH, D_MODEL), 0.05),
        'peer_w_q': nrm(19, (DEPTH, D_MODEL, PEER_HEADS * PEER_QUERY_DIM), D_MODEL ** -0.5),
        'peer_sub_keys': nrm(20, (DEPTH, 2, PEER_N_KEYS, PEER_HALF_DIM), PEER_HALF_DIM ** -0.5),
        'peer_u': nrm(21, (DEPTH, PEER_N_EXPERTS, D_MODEL), D_MODEL ** -0.5),
        'peer_v': nrm(22, (DEPTH, PEER_N_EXPERTS, D_MODEL), 0.5),
        'norm_final_w': 1.0 + nrm(23, (D_MODEL,), 0.05),
    }

def reference(x_prompt, x_sample, state_conv, state_ssm, cache_k_window, cache_v_window,
              norm_mix_w, w_in, conv_w, conv_b, dt_bias, a_log, d_skip, ssm_norm_w, w_ssm_out,
              attn_sinks, w_attn_out, w_out, norm_ffn_w, peer_w_q, peer_sub_keys, peer_u, peer_v,
              norm_final_w):
    yp, ys = x_prompt, x_sample
    conv_p, ssm_p, k_p, v_p = [], [], [], []
    conv_s, ssm_s, k_s, v_s = [], [], [], []
    for i in range(DEPTH):
        lw = {'norm_mix_w': norm_mix_w[i], 'w_in': w_in[i], 'conv_w': conv_w[i], 'conv_b': conv_b[i],
              'dt_bias': dt_bias[i], 'a_log': a_log[i], 'd_skip': d_skip[i], 'ssm_norm_w': ssm_norm_w[i],
              'w_ssm_out': w_ssm_out[i], 'attn_sinks': attn_sinks[i], 'w_attn_out': w_attn_out[i],
              'w_out': w_out[i], 'norm_ffn_w': norm_ffn_w[i], 'peer_w_q': peer_w_q[i],
              'peer_sub_keys': peer_sub_keys[i], 'peer_u': peer_u[i], 'peer_v': peer_v[i]}
        bp = yp.shape[0]
        conv0 = jnp.zeros((bp, SSM_CONV_WIDTH - 1, SSM_CONV_DIM), yp.dtype)
        ssm0 = jnp.zeros((bp, SSM_N_HEADS, SSM_HEAD_DIM, SSM_D_STATE), yp.dtype)
        yp, c1, s1, k1, v1 = trunk_layer(yp, conv0, ssm0, None, None, 0, lw)
        ys, c2, s2, k2, v2 = trunk_layer(ys, state_conv[i], state_ssm[i], cache_k_window[i], cache_v_window[i], PAST_LEN, lw)
        conv_p.append(c1); ssm_p.append(s1); k_p.append(k1); v_p.append(v1)
        conv_s.append(c2); ssm_s.append(s2); k_s.append(k2); v_s.append(v2)
    y_prompt = rms_norm(yp, norm_final_w)
    y_sample = rms_norm(ys, norm_final_w)
    return (y_prompt, y_sample,
            jnp.stack(conv_p), jnp.stack(ssm_p), jnp.stack(k_p), jnp.stack(v_p),
            jnp.stack(conv_s), jnp.stack(ssm_s), jnp.stack(k_s), jnp.stack(v_s))


_drawn_inputs = setup_inputs


def setup_inputs(seed=0):
    import zlib

    import numpy as np

    out = dict(_drawn_inputs(seed))
    spreads = {}
    factors = {'conv_b': 2.679, 'attn_sinks': 8.0}
    for name, (base, spread) in spreads.items():
        noise = np.random.default_rng([zlib.crc32(name.encode()), seed]).standard_normal(out[name].shape)
        drawn = base * np.exp(spread * noise) if base else spread * noise
        out[name] = jnp.asarray(drawn.astype(out[name].dtype))
    for name, factor in factors.items():
        out[name] = (out[name] * factor).astype(out[name].dtype)
    return out
```

```python
from contextlib import ExitStack

import concourse.bass as bass
from concourse import mybir
import numpy as np

F32 = mybir.dt.float32
F32R = mybir.dt.float32r
U32 = mybir.dt.uint32
ALU = mybir.AluOpType
ACT = mybir.ActivationFunctionType
AX = mybir.AxisListType

P = 128
D = 1024
KD = D // P
SEQ = 512
SB, SL = 8, 8
NS = SB * SL
T = SEQ + NS
HT = T // 2
CHUNKS = SEQ // P
NC = CHUNKS + 1
INNER = 2 * D
CI = INNER // P
NH, HP, NG = 32, 64, 8
CB = 2 * NG
CX = CI + CB
AH_, AKV, DH = 16, 4, 64
UNITS = CHUNKS * AKV
WIN = 128
EXPERTS = 16384
ET = EXPERTS // P
PH, TOPK = 8, 16
TB = 64
EPS = 1e-6
NEG = -1e30

N_DT = 0
N_XBC = 1
N_QKV = N_XBC + CX
N_ATT = N_QKV + 12
N_Z = N_ATT + 2 * KD
N_SSM = N_Z + CI
N_OUT = N_SSM + 3 * KD
N_PQ = N_OUT + KD
QUADS = 4
TURNS = T // (4 * QUADS)
ROUTE_U = 6
STORE_U = 6
N_ROUTE = N_PQ + PH + 2 * PH
N_GU = N_ROUTE + NC * ROUTE_U
N_LATE = N_GU + TURNS + STORE_U
EARLY = N_LATE - N_PQ - PH
EP = EARLY // 2
N_MIX = N_LATE + 2 * (EP - 1)
N_ALL = N_PQ + PH + 2 * ET
P_DT, P_XBC, P_QKV, P_ATT, P_Z = N_DT, N_XBC, N_QKV, N_ATT, N_Z
P_SSM = P_Z + CI
P_OUT = P_SSM + 2 * KD
P_PQ = P_OUT + KD
P_SHIFT = N_PQ - P_PQ
P_ROUTE, P_GU, P_LATE = N_ROUTE - P_SHIFT, N_GU - P_SHIFT, N_LATE - P_SHIFT

C_ID, C_TRI, C_BTRI, C_BONE, C_BM, C_IOTA = 0, 128, 256, 320, 384, 392
C_N = C_IOTA + P
Q_MIX, Q_FFN, Q_FIN, Q_CW, Q_CB, Q_SNW, Q_DS, Q_SINK = 0, 8, 16, 24, 152, 184, 200, 216
Q_SSINK, Q_DTB, Q_AL, Q_EPS = 232, 233, 234, 235
Q_N = 236


class Idx:

    def __init__(self, base, i=0, stride=0):
        self.b, self.i, self.s = base, i, stride
        self.par = base % 2
        if isinstance(i, int):
            base, i, stride = base + i * stride, 0, 0
        self.v = base + i * stride if stride else base
        self.half = base // 2 + i * (stride // 2) if stride else base // 2
        self.first = not stride and base < 2


def plus(n, k):
    return Idx(n.b + k, n.i, n.s)


def slot_of(n):
    return n.b % 2 if n.b < N_LATE else (1, 0, 3, 2)[(n.b - N_LATE) % 4]


class Chain:

    def __init__(self, eng, sem):
        self.eng, self.sem, self.base, self.n = eng, sem, 0, 0

    def mark(self, ins):
        ins.then_inc(self.sem, 1)
        self.n += 1

    def wait(self, alone=False):
        self.eng.wait_ge(self.sem, self.base + self.n)
        if alone:
            self.eng.nop(nofuse=True)

    def link(self, ins):
        self.mark(ins)
        self.wait()

    def enter(self, i, first, per):
        self.total, self.per = self.base + self.n, per
        self.base, self.n = i * per + (self.total - first * per), 0

    def leave(self, turns):
        assert self.n == self.per, (self.n, self.per)
        self.base, self.n = self.total + turns * self.per, 0


def at(t, i):
    if isinstance(i, int):
        return t[:, i, :]
    return t[:, bass.ds(i, 1), :].rearrange("p a c -> p (a c)")


def bc(ap, n):
    return ap.unsqueeze(len(ap.shape)).to_broadcast([*ap.shape, n])


def chunk(c):
    return (c * P, P) if not isinstance(c, int) or c < CHUNKS else (SEQ, NS)


def dram(t, i):
    if isinstance(i, int):
        return t[i]
    return t[bass.ds(i, 1)].rearrange("a p c -> (a p) c")


def dram3(t, i):
    if isinstance(i, int):
        return t[:, i]
    return t[:, bass.ds(i, 1)].rearrange("p a i t -> (p a) i t")


def build(nc, xT, wt, consts, params, subk, conv_in, ropes, amask, smask, s_in, kct, kc, vc,
          yT, conv_p, conv_s, ssm_p, ssm_s, kw_p, vw_p, kw_s, vw_s):
    g_dram = nc.dram_tensor("gates_dense", [P, T // TB, P, TB], F32).ap()
    act_dram = nc.dram_tensor("activations_early", [EP, P, 2 * T], F32).ap()

    ctx = ExitStack()
    with ctx:
        base = (nc.sbuf_base + 63) // 64 * 64
        edge = [base]

        def region(nbytes):
            at_ = edge[0]
            edge[0] += (nbytes + 31) // 32 * 32
            assert edge[0] <= nc.sbuf_usable_end, edge[0]
            return [at_, at_ + nbytes]

        def put(reg, name, shape, dt=F32):
            size = 4 * int(np.prod(shape[1:]))
            t = nc.alloc_sbuf_tensor_at(name, shape, dt, offset=reg[0])
            reg[0] += (size + 31) // 32 * 32
            assert reg[0] <= reg[1], name
            return t

        def over(reg, skip=0):
            return [reg[2] + skip, reg[1]]

        def fixed(nbytes):
            r = region(nbytes)
            return r + [r[0]]

        raw_r, split_r = fixed(2 * 4096), fixed(4 * 4096)
        h_r = fixed(2 * 18432)
        x_r = fixed(18432)
        r1, r2, r3 = fixed(36864), fixed(36864), fixed(36864)
        misc = [edge[0], nc.sbuf_usable_end]

        raw = [put(raw_r, f"raw{i}", [P, D]) for i in range(2)]
        whi = [put(split_r, f"whi{i}", [P, KD, P], F32R) for i in range(2)]
        wlo = [put(split_r, f"wlo{i}", [P, KD, P], F32R) for i in range(2)]
        HH = put(h_r, "h_hi", [P, KD, T], F32R)
        HL = put(h_r, "h_lo", [P, KD, T], F32R)
        X = put(x_r, "x", [P, KD, T])
        C = put(misc, "consts_sb", [P, C_N])
        Q = put(misc, "params_sb", [P, Q_N])
        SK = put(misc, "subkeys", [P, P])
        CIN = put(misc, "conv_state_in", [P, CX, SB, 3])
        COP = put(misc, "conv_state_prompt", [P, CX, 3])
        COS_ = put(misc, "conv_state_sample", [P, CX, SB, 3])
        DTK = put(misc, "dt_tok", [P, NC, NH])
        DAK = put(misc, "da_tok", [P, NC, NH])
        ONES = put(misc, "ones", [P, P])
        RINV = put(misc, "rinv", [P, T])
        tmp_at = misc[0]
        TMP = [put(misc, f"tmp{i}", [P, T]) for i in range(2)]
        ident = C[:, C_ID:C_ID + P]
        tri = C[:, C_TRI:C_TRI + P]
        btri = C[:, C_BTRI:C_BTRI + NS]
        bone = C[:, C_BONE:C_BONE + NS]
        bmask = C[:, C_BM:C_BM + SB]
        iota = C[:, C_IOTA:C_IOTA + P]

        q_r = over(r1)
        SQ = [put(q_r, f"sq{i}", [P, T]) for i in range(2)]
        d_r = over(r3)
        DV, DE, DR, DW, DP = [put(d_r, f"dt_work{i}", [P, T]) for i in range(5)]
        NA = put(d_r, "neg_a", [P, 1])
        c_r = over(x_r)
        PB = [put(c_r, f"conv_in_p{i}", [P, 3 + SEQ]) for i in range(2)]
        SBF = [put(c_r, f"conv_in_s{i}", [P, SB, 3 + SL]) for i in range(2)]
        CO = [put(c_r, f"conv_acc{i}", [P, T]) for i in range(2)]
        UX = put(over(r1), "u_x", [P, CI, T])
        UB = put(over(r2), "u_bc", [P, CB, T])
        s_r = over(r3)
        STX = put(s_r, "st_x", [P, CI, P])
        STB = put(s_r, "st_b", [P, NG, P])
        XDT = put(s_r, "xdt", [P, INNER])
        XDD = put(s_r, "xdt_decayed", [P, INNER])
        BTK = put(s_r, "b_tok", [P, NG, P])
        CBM = [put(s_r, f"cb_masked{i}", [P, P]) for i in range(2)]
        DAC = put(s_r, "da_chunk", [P, NH])
        DTC = put(s_r, "dt_chunk", [P, NH])
        AC = put(s_r, "a_cum", [P, NH])
        DIF = put(s_r, "to_end", [P, NH])
        DTE = put(s_r, "dt_to_end", [P, NH])
        CD = put(s_r, "chunk_decay", [P, NH])
        s_r = over(x_r)
        S = put(s_r, "state", [P, INNER])
        SEG = [put(s_r, f"seg{i}", [P, 4, P]) for i in range(2)]
        CE = [put(s_r, f"c_decayed{i}", [P, 4, P]) for i in range(2)]
        s_r = over(x_r)
        S0 = [put(s_r, f"state_s{i}", [P, SB, P]) for i in range(2)]
        S0.append(nc.alloc_sbuf_tensor_at("state_s2", [P, SB, P], F32, offset=tmp_at))
        s_r = over(r3, 8192 * 3 + 4096 * 2 + 1024 + 6 * 128)
        DAM = put(s_r, "da_by_seq", [P, SB, NH])
        CDB = put(s_r, "decay_by_seq", [P, SB, NH])
        s_r = over(r3)
        BMS = [put(s_r, f"b_by_seq{i}", [P, SB, P]) for i in range(2)]
        a_r = over(r3)
        QT = put(a_r, "q", [P, KD, T])
        OH = put(a_r, "o_hi", [P, KD, T], F32R)
        OL = put(over(r3), "o_lo", [P, KD, T], F32R)
        a_r = over(x_r)
        KP = put(a_r, "k_pad", [P, 2, WIN + T])
        VK = put(a_r, "v_tok", [P, NC + 1, AKV * DH])
        VT = [put(a_r, f"v{i}", [P, T]) for i in range(2)]
        a_r = over(x_r, 5632 + 6144)
        KCS = [put(a_r, f"k_cache{i}", [P, 2, P]) for i in range(3)]
        VCS = [put(a_r, f"v_cache{i}", [P, AKV * DH]) for i in range(3)]
        a_r = over(r2)
        CS = put(a_r, "cos_sin", [P, 2, T])
        AM = put(a_r, "mask_prompt", [P, 2, 2 * WIN])
        SM = put(a_r, "mask_sample", [P, SB, WIN + NS])
        QS = put(a_r, "q_sample", [P, 2, KD * SL])
        KCS.append(put(a_r, "k_cache3", [P, 2, P]))
        VCS.append(put(a_r, "v_cache3", [P, AKV * DH]))
        PT = put(a_r, "p_turned", [P, 2, 4 * P])
        rope_at = a_r[0]
        RS = [put(a_r, f"rope_swap{i}", [P, T]) for i in range(2)]
        RT = [put(a_r, f"rope_t{i}", [P, T]) for i in range(2)]
        a_r = [rope_at, r2[1]]
        SC = [put(a_r, f"scores{i}", [P, 4, 2 * WIN]) for i in range(2)]
        AM4 = [put(a_r, f"att_small{i}", [P, 6, 4]) for i in range(2)]
        a_r = over(r2, rope_at - r2[2])
        SCS = [put(a_r, f"scores_s{i}", [P, WIN + NS]) for i in range(2)]
        ATT = put(over(r2), "att", [P, KD, T])
        m_r = over(r2)
        MH = put(m_r, "m_hi", [P, KD, T], F32R)
        ML = put(m_r, "m_lo", [P, KD, T], F32R)
        z_r = over(x_r)
        SQZ = [put(z_r, f"sqz{i}", [P, T]) for i in range(2)]
        ZT = [put(z_r, f"yn{i}", [P, T]) for i in range(2)]
        YH = put(over(r3), "y_hi", [P, CI, T], F32R)
        YL = put(over(r1), "y_lo", [P, CI, T], F32R)
        p_r = over(r1)
        QP = [put(p_r, f"peer_q{i}", [P, T]) for i in range(2)]
        SCO = [put(p_r, f"peer_s{i}", [P, NC, 2, P]) for i in range(2)]
        SCR = [put(p_r, f"peer_rest{i}", [P, P]) for i in range(2)]
        TVH = put(p_r, "top_val_head", [P, NC, 2, TOPK])
        TIH = put(p_r, "top_idx_head", [P, NC, 2, TOPK], U32)
        TV = put(p_r, "top_val", [P, NC, PH, 2, TOPK])
        TI = put(p_r, "top_idx", [P, NC, PH, 2, TOPK])
        p_r = over(r2)
        TVC = put(p_r, "top_val_chunk", [P, PH, 2, TOPK])
        TIC = put(p_r, "top_idx_chunk", [P, PH, 2, TOPK])
        CMB = put(p_r, "combined", [P, PH, TOPK, TOPK])
        CMR = [put(p_r, f"combined_rest{i}", [P, TOPK * TOPK]) for i in range(2)]
        OHT = put(p_r, "onehot_pick", [P, PH, TOPK, TOPK])
        BST = put(p_r, "best", [P, PH, TOPK])
        PCK = put(p_r, "pick", [P, PH, TOPK], U32)
        PAB = put(p_r, "pick_parts", [P, 2, PH * TOPK], U32)
        PAF = put(p_r, "pick_parts_f", [P, 2, PH, TOPK])
        EIJ = put(p_r, "expert_parts", [P, 3, PH * TOPK])
        SUM = put(p_r, "gate_sum", [P, 2, PH])
        g_r = over(r3)
        OJ = [put(g_r, f"onehot_j{i}", [P, 4, P]) for i in range(2 * QUADS)]
        AI = [put(g_r, f"onehot_i{i}", [P, 4, P]) for i in range(2 * QUADS)]
        gb_r = [over(r1)[0], r2[1]]
        GB = [put(gb_r, f"g_block{i}", [P, P, TB]) for i in range(2)]
        EJT = put(gb_r, "expert_turned", [P, 3, T])
        e_r = over(r1)
        whi += [put(e_r, f"whi{i}", [P, KD, P], F32R) for i in (2, 3)]
        wlo += [put(e_r, f"wlo{i}", [P, KD, P], F32R) for i in (2, 3)]
        ACC = put(e_r, "acc", [P, KD, T])
        e_r = over(r2)
        ACH = [put(e_r, f"act_hi{i}", [P, 2, T], F32R) for i in range(2)]
        ACL = [put(e_r, f"act_lo{i}", [P, 2, T], F32R) for i in range(2)]
        GE = [put(e_r, f"gelu{i}", [P, 2, T]) for i in range(2)]
        G2 = [put(e_r, f"g_tile{i}", [P, T // TB, 2, TB]) for i in range(2)]
        PS = [ctx.enter_context(nc.psum_tensor(f"ps{i}", [P, 512], F32)) for i in range(8)]

        def sem(name):
            return ctx.enter_context(nc.semaphore(name))

        x_in, const_in, small_in = sem("x_in"), sem("const_in"), sem("small_in")
        rope_in, mask_in, x_again = sem("rope_in"), sem("mask_in"), sem("x_again")
        s0_in = [sem(f"s0_in{i}") for i in range(3)]
        s0_out = [sem(f"s0_out{i}") for i in range(3)]
        cache_in = [sem(f"cache_in{i}") for i in range(4)]
        g_in = [sem(f"g_in{i}") for i in range(2)]
        act_in = [sem(f"act_in{i}") for i in range(2)]
        act_out = [sem(f"act_out{i}") for i in range(2)]
        g_out = [sem(f"g_out{i}") for i in range(2)]
        raw_in = [sem(f"raw_in{i}") for i in range(2)]
        stored, ssm_stored = sem("stored"), sem("ssm_stored")
        hi_done, split_ready, tile_done = sem("hi_done"), sem("split_ready"), sem("tile_done")
        slot_used = [sem(f"slot_used{i}") for i in range(2)]
        setup = sem("setup")
        sq_ready, sq_used, std_ready = sem("sq_ready"), sem("sq_used"), sem("std_ready")
        h_ready = sem("h_ready")
        dve_own = sem("dve_own")
        dt_v, dt_abs, dt_exp, dt_ready, dtt_ready, dtk_ready = [
            sem(n) for n in ("dt_v", "dt_abs", "dt_exp", "dt_ready", "dtt_ready", "dtk_ready")]
        conv_done, silu_done = sem("conv_done"), sem("silu_done")
        staged, acum_ready, diff_ready, dexp_ready = [
            sem(n) for n in ("staged", "acum_ready", "diff_ready", "dexp_ready")]
        turned, turned_used = sem("turned"), sem("turned_used")
        acb_ready, cb_ready, seg_ready, e_ready, ec_ready, mt_ready = [
            sem(n) for n in ("acb_ready", "cb_ready", "seg_ready", "e_ready", "ec_ready", "mt_ready")]
        y_ready, y_used, cs_ready, cs_used = [sem(n) for n in ("y_ready", "y_used", "cs_ready", "cs_used")]
        bms_ready = sem("bms_ready")
        rs_ready, rope_done, v_ready, v_turned, v_tok = [
            sem(n) for n in ("rs_ready", "rope_done", "v_ready", "v_turned", "v_tok")]
        blk_staged, sc_ready, m_ready, p_exp, p_ready = [
            sem(n) for n in ("blk_staged", "sc_ready", "m_ready", "p_exp", "p_ready")]
        sc_used = sem("sc_used")
        pt_ready, pt_copied, pv_ready, o_done = [
            sem(n) for n in ("pt_ready", "pt_copied", "pv_ready", "o_done")]
        zs_ready, yz_ready, zsq_ready, zsq_used, zstd, yn_done = [
            sem(n) for n in ("zs_ready", "yz_ready", "zsq_ready", "zsq_used", "zstd", "yn_done")]
        merged = sem("merged")
        score_ready, score_copied, head_done = [
            sem(n) for n in ("score_ready", "score_copied", "head_done")]
        gmax, gexp, parts_ready, parts_turned, routed = [
            sem(n) for n in ("gmax", "gexp", "parts_ready", "parts_turned", "routed")]
        hot_ready, g_ready, g_copied = sem("hot_ready"), sem("g_ready"), sem("g_copied")
        gelu_ready, act_ready, out_ready, acc_done = [
            sem(n) for n in ("gelu_ready", "act_ready", "out_ready", "acc_done")]
        y_done = sem("y_done")

        block = ctx.enter_context(nc.Block())

        @block.sync
        def _(sp):
            def load(n, src):
                if not n.first:
                    sp.wait_ge(split_ready, n.v - 1)
                sp.dma_start(raw[n.par][:, :], src).then_inc(raw_in[n.par], 16)

            for k in range(2):
                load(Idx(k), dram(wt, k))
            with sp.Fori(1, N_ALL // 2) as i:
                for k in range(2):
                    n = Idx(k, i, 2)
                    load(n, dram(wt, n.v))
            load(Idx(N_ALL - 1), dram(wt, N_ALL - 1))

        @block.gpsimd
        def _(pool):
            def low(n):
                slot = slot_of(n)
                pool.wait_ge(hi_done, n.v + 1)
                hi = whi[slot][:, :, :].rearrange("p k c -> p (k c)")
                lo = wlo[slot][:, :, :].rearrange("p k c -> p (k c)")
                pool.tensor_tensor(lo, raw[n.par][:, :], hi.bitcast(F32), ALU.subtract).then_inc(split_ready, 1)

            with pool.Fori(0, N_LATE // 2) as i:
                for k in range(2):
                    low(Idx(k, i, 2))
            low(Idx(N_LATE - 1))
            with pool.Fori(0, (N_ALL - N_LATE) // 4) as i:
                for k in range(4):
                    low(Idx(N_LATE + k, i, 4))

        @block.tensor
        def _(pe):
            def project(n, p, xh, xl, k0=0, first=True, last=True, norm=None):
                slot = slot_of(n)
                pe.wait_ge(split_ready, n.v + 1)
                if first and not p.first:
                    pe.wait_ge(slot_used[p.par], p.half)
                for k in range(KD):
                    if norm is not None:
                        pe.wait_ge(h_ready, norm * KD + k + 1)
                    for w, x in ((whi, xh), (whi, xl), (wlo, xh)):
                        for h in range(2):
                            mm = pe.matmul(PS[2 * p.par + h][:, 0:HT], w[slot][:, k, :],
                                           x[:, k0 + k, h * HT:(h + 1) * HT],
                                           start=first and k == 0 and w is whi and x is xh,
                                           stop=last and k == KD - 1 and w is wlo)
                mm.then_inc(tile_done, 1)

            def square_sum(count, buf, start=False, stop=False):
                pe.wait_ge(sq_ready, count + 1)
                for h in range(2):
                    mm = pe.matmul(PS[4 + h][:, 0:HT], ONES[:, :], SQ[buf][:, h * HT:(h + 1) * HT],
                                   start=start, stop=stop)
                mm.then_inc(sq_used, 1)

            def square_sums(turn):
                for k in range(KD):
                    square_sum(turn * KD + k, k % 2, start=k == 0, stop=k == KD - 1)

            pe.wait_ge(setup, 1)
            pe.wait_ge(const_in, 16)
            square_sums(0)
            project(Idx(N_DT), Idx(P_DT), HH, HL, norm=0)
            for k in range(2):
                project(Idx(N_XBC + k), Idx(P_XBC + k), HH, HL)
            with pe.Fori(1, CX // 2) as i:
                for k in range(2):
                    project(Idx(N_XBC + k, i, 2), Idx(P_XBC + k, i, 2), HH, HL)
            pe.wait_ge(dt_ready, 1)
            for c in range(NC):
                t0, L = chunk(c)
                pe.transpose(PS[6][0:L, c * NH:(c + 1) * NH], DP[0:NH, t0:t0 + L], ident[0:NH, 0:NH])
                mm = pe.transpose(PS[6][0:L, (NC + c) * NH:(NC + c + 1) * NH], DR[0:NH, t0:t0 + L],
                                  ident[0:NH, 0:NH])
            mm.then_inc(dtt_ready, 1)

            def ssd(c):
                t0, L = chunk(c)
                sample = isinstance(c, int) and c == CHUNKS
                start = isinstance(c, int) and c == 0
                csum = btri[0:L, :] if sample else tri
                u0 = c * NG
                pe.wait_ge(staged, c + 1)
                pe.matmul(PS[2][0:L, 0:NH], csum, DAC[0:L, :], start=True, stop=True)
                mm = pe.matmul(PS[3][0:L, 0:NH], bone[0:L, :] if sample else ONES[0:L, :], DAC[0:L, :],
                               start=True, stop=True)
                if sample:
                    mm = pe.matmul(PS[3][:, NH:NH + SB * NH], ONES[0:L, :],
                                   DAM[0:L, :, :].rearrange("p b h -> p (b h)"), start=True, stop=True)
                mm.then_inc(acum_ready, 1)
                for q in range(6):
                    if q >= 2:
                        pe.wait_ge(turned_used, c * 6 + q - 1)
                    elif not start:
                        pe.wait_ge(cs_used, u0)
                    for k in range(4):
                        src = STX[:, 4 * q + k, 0:L] if q < 4 else STB[:, 4 * (q - 4) + k, 0:L]
                        mm = pe.transpose(PS[6 + q % 2][0:L, k * P:(k + 1) * P], src, ident)
                    mm.then_inc(turned, 1)
                pe.wait_ge(turned_used, c * 6 + 6)

                def new_states(g, pair):
                    hs = (4 * g + 2 * pair) * HP
                    for half in range(2):
                        q = 4 * g + 2 * pair + half
                        if q >= 2:
                            pe.wait_ge(cs_used, NG * CHUNKS + q - 1)
                        for b in range(4):
                            mm = pe.matmul(PS[6 + half][:, b * P:(b + 1) * P],
                                           BMS[g % 2][0:NS, 4 * half + b, :], XDD[0:NS, hs:hs + P],
                                           start=True, stop=True)
                        mm.then_inc(cs_ready, 1)

                def front(g):
                    u = u0 + g
                    if not start or g >= 2:
                        pe.wait_ge(cb_ready, u - 1)
                        pe.wait_ge(seg_ready, u - 1)
                        pe.wait_ge(ec_ready, u - 1)
                    for r in range(4):
                        pe.matmul(PS[g % 2][:, r * P:r * P + L],
                                  DAC[0:L, 4 * g + r:4 * g + r + 1].to_broadcast([L, P]), csum,
                                  start=True, stop=True)
                    pe.matmul(PS[2 + g % 2][0:L, 0:L], STB[:, g, 0:L], UB[:, NG + g, bass.ds(t0, L)],
                              start=True, stop=True).then_inc(acb_ready, 1)

                def back(g):
                    u = u0 + g
                    if sample:
                        pe.wait_ge(bms_ready, g + 1)
                        new_states(g, 0)
                    else:
                        if g >= 2:
                            pe.wait_ge(cs_used, u - 1)
                        pe.matmul(PS[6 + g % 2][:, 0:4 * HP], BTK[:, g, :], XDD[:, 4 * g * HP:4 * (g + 1) * HP],
                                  start=True, stop=True).then_inc(cs_ready, 1)
                    pe.wait_ge(mt_ready, u + 1)
                    if not start or g >= 2:
                        pe.wait_ge(y_used, u - 1)
                    if not start and not sample:
                        pe.wait_ge(cs_used, u - NG + 1)
                    for r in range(4):
                        h = 4 * g + r
                        out = PS[4 + g % 2][64 * (r % 2):64 * (r % 2) + 64, P * (r // 2):P * (r // 2) + L]
                        pe.matmul(out, XDT[0:L, h * HP:(h + 1) * HP], SEG[g % 2][0:L, r, 0:L],
                                  start=True, stop=False, skip_group_check=sample)
                        if not sample:
                            mm = pe.matmul(out, S[:, h * HP:(h + 1) * HP], CE[g % 2][:, r, 0:L],
                                           start=False, stop=True)
                            continue
                        if r % 2 == 0:
                            v = 2 * g + r // 2
                            pe.wait_ge(s0_in[v % 3], 16 * (v // 3 + 1))
                        for b in range(SB):
                            mm = pe.matmul(out[:, SL * b:SL * (b + 1)],
                                           S0[v % 3][:, b, HP * (r % 2):HP * (r % 2 + 1)],
                                           CE[g % 2][:, r, SL * b:SL * (b + 1)],
                                           start=False, stop=True, skip_group_check=True)
                    mm.then_inc(y_ready, 1)

                front(0)
                if sample:
                    front(1)
                    for g in range(NG):
                        back(g)
                        if g < NG - 2:
                            front(g + 2)
                        new_states(g, 1)
                    return
                for g in range(NG):
                    if g < NG - 1:
                        front(g + 1)
                    back(g)

            ssd(0)
            with pe.Fori(1, CHUNKS) as c:
                ssd(c)
            ssd(CHUNKS)
            pe.wait_ge(y_used, NC * NG)

            for k in range(2):
                project(Idx(N_QKV + k), Idx(P_QKV + k), HH, HL)
            with pe.Fori(1, 6) as i:
                for k in range(2):
                    project(Idx(N_QKV + k, i, 2), Idx(P_QKV + k, i, 2), HH, HL)
            for k in (10, 11):
                p = Idx(P_QKV + k)
                pe.wait_ge(slot_used[p.par], p.half + 1)
            pe.wait_ge(rope_done, 10)
            for c in range(NC):
                t0, L = chunk(c)
                for k in range(2):
                    lo = (c % 2) * 2 * P + k * P
                    pe.transpose(PS[4 + c // 2][0:L, lo:lo + P], VT[k][:, t0:t0 + L], ident)
            for k in range(2):
                pe.transpose(PS[7][:, k * P:(k + 1) * P], KP[:, k, SEQ:SEQ + WIN], ident)
                mm = pe.transpose(PS[7][0:NS, (2 + k) * P:(3 + k) * P], KP[:, k, WIN + SEQ:WIN + T], ident)
            mm.then_inc(v_turned, 1)

            def scores(u):
                n, g = divmod(u, AKV)
                if u >= 2:
                    pe.wait_ge(sc_used, u - 1)
                a = 64 * (g % 2)
                for r in range(4):
                    lo = (r % 2) * 2 * WIN
                    mm = pe.matmul(PS[2 * (g % 2) + r // 2][:, lo:lo + 2 * WIN],
                                   QT[a:a + 64, (g // 2) * 4 + r, n * P:(n + 1) * P],
                                   KP[a:a + 64, g // 2, n * P:n * P + 2 * WIN], start=True, stop=True)
                mm.then_inc(sc_ready, 1)

            def turn(u):
                pe.wait_ge(p_ready, u + 1)
                if u >= 1:
                    pe.wait_ge(pt_copied, u)
                for half in range(2):
                    for r in range(4):
                        mm = pe.transpose(PS[4 + half][:, r * P:(r + 1) * P],
                                          SC[u % 2][:, r, half * WIN:(half + 1) * WIN], ident)
                mm.then_inc(pt_ready, 1)

            def values(u):
                n, g = divmod(u, AKV)
                pe.wait_ge(pt_copied, u + 1)
                if n and g % 2 == 0:
                    pe.wait_ge(o_done, n * 2 + g // 2 - 1)
                a = 64 * (g % 2)
                for half in range(2):
                    mm = pe.matmul(PS[6 + g // 2][a:a + 64, :], VK[:, n + half, g * DH:(g + 1) * DH],
                                   PT[:, half, :], start=half == 0, stop=half == 1)
                mm.then_inc(pv_ready, 1)

            pe.wait_ge(v_tok, 1)
            for u in range(2):
                scores(u)
            for u in range(UNITS):
                turn(u)
                if u < UNITS - 2:
                    scores(u + 2)
                values(u)

            pe.wait_ge(pt_copied, UNITS)

            def attend_pair(i, j):
                for k in range(2):
                    b, c = i * 4 + (2 * j + k), 2 * j + k
                    u = b + UNITS
                    pe.wait_ge(blk_staged, b + 1)
                    pe.wait_ge(cache_in[c], i * 32 + 32)
                    pe.wait_ge(sc_used, u - 1)
                    pe.nop(nofuse=True)
                    for g in range(AKV):
                        a, o = 64 * (g % 2), 32 * g
                        lhs = QS[a:a + 64, k, (g // 2) * 32:(g // 2) * 32 + 32]
                        pe.matmul(PS[2 * k][o:o + 32, 0:WIN], lhs, KCS[c][a:a + 64, g // 2, :],
                                  start=True, stop=True)
                        mm = pe.matmul(PS[2 * k][o:o + 32, WIN:WIN + NS], lhs,
                                       KP[a:a + 64, g // 2, WIN + SEQ:WIN + T], start=True, stop=True)
                    mm.then_inc(sc_ready, 1)
                for k in range(2):
                    u = i * 4 + (2 * j + k + UNITS)
                    pe.wait_ge(p_ready, u + 1)
                    pe.wait_ge(pt_copied, u - 1)
                    pe.transpose(PS[4 + k][:, 0:P], SCS[k][:, 0:WIN], ident)
                    pe.transpose(PS[4 + k][0:NS, P:2 * P], SCS[k][:, WIN:WIN + NS], ident).then_inc(pt_ready, 1)
                for k in range(2):
                    b, c = i * 4 + (2 * j + k), 2 * j + k
                    pe.wait_ge(pt_copied, b + (UNITS + 1))
                    pe.wait_ge(o_done, b + 7)
                    for g in range(AKV):
                        a, o, q = 64 * (g % 2), 32 * (g // 2), P * k + 32 * g
                        out = PS[6 + k][a:a + 64, o:o + 32]
                        pe.matmul(out, VCS[c][:, g * DH:(g + 1) * DH], PT[:, 0, q:q + 32],
                                  start=True, stop=False)
                        mm = pe.matmul(out, VK[0:NS, NC, g * DH:(g + 1) * DH], PT[0:NS, 1, q:q + 32],
                                       start=False, stop=True)
                    mm.then_inc(pv_ready, 1)

            with pe.Fori(0, SB // 4) as i:
                for j in range(2):
                    attend_pair(i, j)

            pe.wait_ge(o_done, 16)
            with pe.Fori(0, KD) as i:
                project(Idx(N_ATT, i, 2), Idx(P_ATT, i, 2), HH, HL)
                project(Idx(N_ATT + 1, i, 2), Idx(P_ATT + 1, i, 2), OH, OL)

            def group_sums(g, first=False):
                pe.wait_ge(zsq_ready, g * 2 + 2)
                if not first:
                    pe.wait_ge(zstd, g)
                for k in range(2):
                    for h in range(2):
                        mm = pe.matmul(PS[4 + h][:, 0:HT], ONES[:, :], SQZ[k][:, h * HT:(h + 1) * HT],
                                       start=k == 0, stop=k == 1)
                    mm.then_inc(zsq_used, 1)

            for g in range(2):
                for k in range(2):
                    project(Idx(N_Z + 2 * g + k), Idx(P_Z + 2 * g + k), HH, HL)
            group_sums(0, first=True)
            with pe.Fori(2, NG) as g:
                for k in range(2):
                    project(Idx(N_Z + k, g, 2), Idx(P_Z + k, g, 2), HH, HL)
                group_sums(g - 1)
            group_sums(NG - 1)

            with pe.Fori(0, KD // 2) as i:
                for j in range(2):
                    n = [Idx(N_SSM + 3 * j + k, i, 6) for k in range(3)]
                    project(n[0], Idx(P_SSM + 2 * j, i, 4), HH, HL)
                    p = Idx(P_SSM + 2 * j + 1, i, 4)
                    if j == 0:
                        pe.wait_ge(yn_done, NG // 2)
                    project(n[1], p, YH, YL, last=False)
                    if j == 0:
                        pe.wait_ge(yn_done, NG)
                    project(n[2], p, YH, YL, k0=KD, first=False)
            pe.wait_ge(merged, KD)
            for k in range(2):
                project(Idx(N_OUT + k), Idx(P_OUT + k), MH, ML)
            square_sum(KD, 0, start=True)
            with pe.Fori(1, KD // 2) as i:
                for k in range(2):
                    project(Idx(N_OUT + k, i, 2), Idx(P_OUT + k, i, 2), MH, ML)
                    square_sum(i * 2 + (KD - 1 + k), 1 - k)
            square_sum(2 * KD - 1, 1, stop=True)

            def key_scores(h, k, p, first=False):
                pe.wait_ge(slot_used[p.par], p.half + 1)
                if not first:
                    pe.wait_ge(score_copied, h)
                for c in range(NC):
                    t0, L = chunk(c)
                    for j in range(2):
                        lo = c % CHUNKS * P
                        mm = pe.matmul(PS[4 + j + 2 * (c // CHUNKS)][0:L, lo:lo + P],
                                       QP[k][64 * j:64 * j + 64, t0:t0 + L],
                                       SK[64 * j:64 * j + 64, :], start=True, stop=True)
                mm.then_inc(score_ready, 1)

            def single(n, norm=None):
                project(n, plus(n, -P_SHIFT), HH, HL, norm=norm)

            for k in range(2):
                single(Idx(N_PQ + k), norm=1 - k or None)
            key_scores(0, 0, Idx(P_PQ), first=True)
            for k in range(2):
                single(Idx(N_PQ + 2 + k))
            key_scores(1, 1, Idx(P_PQ + 1))
            single(Idx(N_PQ + 4))
            with pe.Fori(0, 2) as i:
                for j in range(2):
                    n = Idx(N_PQ + 5 + 3 * j, i, 6)
                    single(n)
                    single(plus(n, 1))
                    key_scores(i * 2 + (2 + j), j, plus(n, -1 - P_SHIFT))
                    single(plus(n, 2))
            for j in range(2):
                n = Idx(N_PQ + 17 + 3 * j)
                single(n)
                single(plus(n, 1))
                key_scores(6 + j, j, plus(n, -1 - P_SHIFT))
                if j == 0:
                    single(plus(n, 2))
            for k in range(2):
                single(Idx(N_ROUTE - 2 + k))

            def turn_parts(c):
                t0, L = chunk(c)
                first = isinstance(c, int) and c == 0
                for k in range(ROUTE_U):
                    single(Idx(N_ROUTE + k, c, ROUTE_U))
                pe.wait_ge(parts_ready, c + 1)
                if not first:
                    pe.wait_ge(routed, c)
                for s in range(3):
                    mm = pe.transpose(PS[7][:, s * P:s * P + L], EIJ[0:L, s, :], ident[0:L, 0:L])
                mm.then_inc(parts_turned, 1)

            turn_parts(0)
            with pe.Fori(1, CHUNKS) as c:
                turn_parts(c)
            turn_parts(CHUNKS)

            def gates(t, par, first=False):
                for k in range(QUADS):
                    pe.wait_ge(hot_ready, t * QUADS + (k + 1))
                    if not first:
                        pe.wait_ge(g_copied, t * QUADS + (k + 1 - QUADS))
                    elif k == 3:
                        pe.wait_ge(routed, NC)
                    buf = par * QUADS + k
                    for q in range(4):
                        mm = pe.matmul(PS[4 + k][:, q * P:(q + 1) * P], OJ[buf][:, q, :], AI[buf][:, q, :],
                                       start=True, stop=True)
                    mm.then_inc(g_ready, 1)

            for j in range(2):
                gates(j, j, first=j == 0)
                single(Idx(N_GU + j))
            with pe.Fori(1, TURNS // 2) as i:
                for j in range(2):
                    gates(i * 2 + j, j)
                    single(Idx(N_GU + j, i, 2))
            for k in range(STORE_U):
                single(Idx(N_GU + TURNS + k))

            def down(it, n, buf, first=False):
                pe.wait_ge(split_ready, n.v + 2)
                pe.wait_ge(act_ready, it * 2 + 2)
                for q in range(2 * KD):
                    d, h = q // 2, q % 2
                    if not first or q >= 4:
                        pe.wait_ge(acc_done, it * 16 + (q - 3))
                    for k in range(2):
                        s = slot_of(plus(n, k))
                        for w, x in ((whi, ACH), (whi, ACL), (wlo, ACH)):
                            mm = pe.matmul(PS[4 + q % 4][:, 0:HT], w[s][:, d, :],
                                           x[buf][:, k, h * HT:(h + 1) * HT],
                                           start=k == 0 and w is whi and x is ACH, stop=k == 1 and w is wlo)
                        if q == 2 * KD - 1:
                            mm.then_inc(tile_done, 1)
                    if q < 2 * KD - 1:
                        mm.then_inc(out_ready, 1)

            down(0, Idx(N_LATE), 0, first=True)
            with pe.Fori(0, (EP - 2) // 2) as i:
                for j in range(2):
                    down(i * 2 + (1 + j), Idx(N_LATE + 2 + 2 * j, i, 4), 1 - j)
            def both(it, i, j):
                n, p = Idx(N_MIX + 4 * j, i, 8), Idx(P_LATE + 2 * j, i, 4)
                for k in range(2):
                    project(plus(n, k), plus(p, k), HH, HL)
                down(it, plus(n, 2), 1 - j)

            with pe.Fori(0, (ET // 2 - EP) // 2) as i:
                for j in range(2):
                    both(i * 2 + (EP - 1 + j), i, j)
            down(ET // 2 - 1, Idx(N_ALL - 2), 1)
            square_sums(2)

        @block.scalar
        def _(act):
            def halves(dst, p, func, **kw):
                for h in range(2):
                    ins = act.activation(dst[:, h * HT:(h + 1) * HT], PS[2 * p.par + h][:, 0:HT], func, **kw)
                return ins

            def norm(turn, src, before=None):
                for k in range(KD):
                    if before:
                        before(k)
                    if k >= 2:
                        act.wait_ge(sq_used, turn * KD + k - 1)
                    act.activation(SQ[k % 2][:, :], src[:, k, :], ACT.Square).then_inc(sq_ready, 1)
                act.wait_ge(sq_used, (turn + 1) * KD)
                for h in range(2):
                    ins = act.activation(TMP[0][:, h * HT:(h + 1) * HT], PS[4 + h][:, 0:HT], ACT.Sqrt,
                                         bias=Q[:, Q_EPS:Q_EPS + 1], scale=1.0 / D)
                ins.then_inc(std_ready, 1)

            act.dma_start(X[:, :, :], xT.rearrange("p (k t) -> p k t", k=KD)).then_inc(x_in, 16)
            act.dma_start(Q[:, :], params).then_inc(small_in, 16)
            act.dma_start(CIN[:, :, :, :], conv_in.rearrange("p (c b j) -> p c b j", c=CX, b=SB))\
                .then_inc(small_in, 16)
            act.dma_start(SK[:, :], subk).then_inc(small_in, 16)
            act.dma_start(C[:, :], consts).then_inc(const_in, 16)
            act.dma_start(kw_s[:, 0:WIN - SL, :], kc[:, SL:WIN, :]).then_inc(stored, 16)
            act.dma_start(vw_s[:, 0:WIN - SL, :], vc[:, SL:WIN, :]).then_inc(stored, 16)
            def high(n, lag=2):
                slot = slot_of(n)
                if lag:
                    act.wait_ge(tile_done, n.v - lag + 1)
                act.wait_ge(raw_in[n.par], n.half * 16 + 16)
                act.activation(whi[slot][:, :, :].rearrange("p k c -> p (k c)"), raw[n.par][:, :], ACT.Copy)\
                    .then_inc(hi_done, 1)

            for k in range(2):
                high(Idx(k), lag=0)
            act.wait_ge(x_in, 16)
            act.wait_ge(small_in, 48)
            norm(0, X)

            high(Idx(2))
            for h in range(2):
                ins = act.activation(DV[0:NH, h * HT:(h + 1) * HT], PS[h][0:NH, 0:HT], ACT.Identity,
                                     bias=Q[0:NH, Q_DTB:Q_DTB + 1])
            ins.then_inc(slot_used[0], 1)
            act.activation(NA[0:NH, :], Q[0:NH, Q_AL:Q_AL + 1], ACT.Exp)
            act.wait_ge(dt_abs, 1)
            act.activation(DR[0:NH, :], DE[0:NH, :], ACT.Exp, scale=-1.0).then_inc(dt_exp, 1)

            def fill(n, m, k, first=False):
                high(plus(n, 2))
                if not first:
                    act.wait_ge(conv_done, m - 1)
                lo, hi = PS[2 * n.par], PS[2 * n.par + 1]
                act.activation(PB[k][:, 3:3 + HT], lo[:, 0:HT], ACT.Copy)
                act.activation(PB[k][:, 3 + HT:3 + SEQ], hi[:, 0:SEQ - HT], ACT.Copy)
                act.activation(SBF[k][:, :, 3:3 + SL],
                               hi[:, SEQ - HT:HT].rearrange("p (b j) -> p b j", b=SB), ACT.Copy)\
                    .then_inc(slot_used[n.par], 1)

            def silu(dst, m, k, done):
                act.wait_ge(conv_done, done)
                act.activation(at(dst, m), CO[k][:, :], ACT.Silu).then_inc(silu_done, 1)

            def conv_pair(i, tile0, fst, prev):
                for k in range(2):
                    n = Idx(N_XBC + k, i, 2)
                    fill(n, i * 2 + k, k, first=fst)
                    if k == 1 or prev is not None:
                        dst, off = (prev if k == 0 else tile0)
                        silu(dst, i * 2 + (k - 1) - off, 1 - k, i * 2 + k)

            conv_pair(0, (UX, 0), True, None)
            with act.Fori(1, CI // 2) as i:
                conv_pair(i, (UX, 0), False, (UX, 0))
            conv_pair(CI // 2, (UB, CI), False, (UX, 0))
            with act.Fori(CI // 2 + 1, CX // 2) as i:
                conv_pair(i, (UB, CI), False, (UB, CI))
            silu(UB, CB - 1, 1, CX)
            act.dma_start(conv_p, COP[:, :, :].rearrange("p c j -> p (c j)")).then_inc(stored, 16)
            act.dma_start(conv_s, COS_[:, :, :, :].rearrange("p c b j -> p (c b j)")).then_inc(stored, 16)

            def ssd(c):
                t0, L = chunk(c)
                sample = isinstance(c, int) and c == CHUNKS
                start = isinstance(c, int) and c == 0
                u0 = c * NG
                act.wait_ge(diff_ready, c + 1)
                act.activation(DTE[0:L, :], DIF[0:L, :], ACT.Exp)
                if sample:
                    ins = act.activation(CDB[:, :, :].rearrange("p b h -> p (b h)"),
                                         PS[3][:, NH:NH + SB * NH], ACT.Exp)
                else:
                    ins = act.activation(CD[:, :], PS[3][:, 0:NH], ACT.Exp)
                ins.then_inc(dexp_ready, 1)
                def exps(g):
                    u = u0 + g
                    act.wait_ge(acb_ready, u + 1)
                    if g >= 2 or not start:
                        act.wait_ge(y_ready, u - 1)
                    for r in range(4):
                        h = 4 * g + r
                        ins = act.activation(SEG[g % 2][0:L, r, 0:L], PS[g % 2][0:L, r * P:r * P + L], ACT.Relu,
                                             bias=AC[0:L, h:h + 1], scale=-1.0)
                    ins.then_inc(seg_ready, 1)
                    act.activation(CE[g % 2][:, :, 0:L],
                                   PS[g % 2][:, :].rearrange("p (r t) -> p r t", r=4)[:, :, 0:L],
                                   ACT.Exp).then_inc(ec_ready, 1)
                    act.wait_ge(seg_ready, u + 1)
                    act.activation(SEG[g % 2][0:L, :, 0:L], SEG[g % 2][0:L, :, 0:L], ACT.Exp, scale=-1.0)\
                        .then_inc(e_ready, 1)

                def move_states(v):
                    act.wait_ge(cs_used, CHUNKS * NG + 2 * v + 2)
                    act.dma_start(ssm_s[v, :, :], S0[v % 3][:, :, :].rearrange("p b c -> p (b c)"))\
                        .then_inc(s0_out[v % 3], 16)
                    if 1 <= v < 2 * NG - 2:
                        act.wait_ge(s0_out[(v - 1) % 3], 16 * ((v - 1) // 3 + 1))
                        load_states(v + 2)

                exps(0)
                for g in range(NG):
                    if g < NG - 1:
                        exps(g + 1)
                    if sample:
                        for w in range(2):
                            move_states(2 * g + w)

            def load_states(v):
                act.dma_start(S0[v % 3][:, :, :].rearrange("p b c -> p (b c)"), s_in[v, :, :])\
                    .then_inc(s0_in[v % 3], 16)

            ssd(0)
            with act.Fori(1, CHUNKS) as c:
                ssd(c)
            act.wait_ge(cs_used, CHUNKS * NG)
            act.dma_start(ssm_p, S[:, :]).then_inc(ssm_stored, 16)
            act.wait_ge(ssm_stored, 16)
            act.wait_ge(y_used, CHUNKS * NG)
            for v in range(3):
                load_states(v)
            ssd(CHUNKS)
            act.wait_ge(y_used, NC * NG)
            for w in range(3):
                act.wait_ge(s0_out[w], 16 * ((2 * NG - 1 - w) // 3 + 1))
            act.dma_start(CS[:, :, :], ropes.rearrange("p (s t) -> p s t", s=2)).then_inc(rope_in, 16)
            act.dma_start(AM[:, :, :], amask.rearrange("p (s t) -> p s t", s=2)).then_inc(mask_in, 16)
            act.dma_start(SM[:, :, :], smask.rearrange("p (s t) -> p s t", s=SB)).then_inc(mask_in, 16)

            def swap(n, m, k, first=False):
                high(plus(n, 2))
                if not first:
                    act.wait_ge(rope_done, m - 1)
                for h in range(2):
                    for q in range(4):
                        o = 32 * (q ^ 1)
                        ins = act.activation(RS[k][32 * q:32 * q + 32, h * HT:(h + 1) * HT],
                                             PS[2 * n.par + h][o:o + 32, 0:HT], ACT.Copy)
                ins.then_inc(rs_ready, 1)

            for k in range(2):
                swap(Idx(N_QKV + k), k, k, first=True)
            with act.Fori(1, 5) as i:
                for k in range(2):
                    swap(Idx(N_QKV + k, i, 2), i * 2 + k, k)
            for k in range(2):
                n = Idx(N_QKV + 10 + k)
                high(plus(n, 2))
                halves(VT[k], n, ACT.Copy).then_inc(slot_used[n.par], 1)
            def load_cache(b):
                act.dma_start(KCS[b % 4][:, :, :].rearrange("p s c -> p (s c)"), kct[b])\
                    .then_inc(cache_in[b % 4], 16)
                act.dma_start(VCS[b % 4][:, :], vc[b]).then_inc(cache_in[b % 4], 16)

            act.wait_ge(v_tok, 1)
            for b in range(4):
                load_cache(b)

            def weights(u):
                A = AM4[u % 2]
                act.wait_ge(m_ready, u + 1)
                for r in range(4):
                    act.activation(SC[u % 2][:, r, :], SC[u % 2][:, r, :], ACT.Exp, bias=A[:, 2, r:r + 1],
                                   scale=DH ** -0.5, accum_out=A[:, 4, r:r + 1])
                act.activation(A[:, 5, :], A[:, 3, :], ACT.Exp).then_inc(p_exp, 1)

            def take(u):
                act.wait_ge(pt_ready, u + 1)
                if u >= 1:
                    act.wait_ge(pv_ready, u)
                act.activation(PT[:, 0, :], PS[4][:, :], ACT.Copy)
                act.activation(PT[:, 1, :], PS[5][:, :], ACT.Copy).then_inc(pt_copied, 1)

            for u in range(2):
                weights(u)
            for u in range(UNITS):
                take(u)
                if u < UNITS - 2:
                    weights(u + 2)
            ktok = TMP[0]
            act.dma_start(kw_p, ktok[:, 0:2 * P]).then_inc(stored, 16)
            act.dma_start(vw_p, VK[:, CHUNKS, :]).then_inc(stored, 16)
            for b in range(SB):
                rows = slice(b * SL, (b + 1) * SL)
                act.dma_start(kw_s[b, WIN - SL:WIN, :], ktok[rows, 2 * P:4 * P]).then_inc(stored, 16)
                act.dma_start(vw_s[b, WIN - SL:WIN, :], VK[rows, NC, :]).then_inc(stored, 16)

            def attend_pair(i, j):
                for k in range(2):
                    u = i * 4 + (2 * j + k + UNITS)
                    A = AM4[k]
                    act.wait_ge(m_ready, u + 1)
                    act.activation(SCS[k][:, :], SCS[k][:, :], ACT.Exp, bias=A[:, 2, 0:1],
                                   scale=DH ** -0.5, accum_out=A[:, 4, 0:1])
                    act.activation(A[:, 5, 0:1], A[:, 3, 0:1], ACT.Exp).then_inc(p_exp, 1)
                for k in range(2):
                    u = i * 4 + (2 * j + k + UNITS)
                    act.wait_ge(pt_ready, u + 1)
                    act.wait_ge(pv_ready, u - 1)
                    act.activation(PT[:, 0, P * k:P * k + P], PS[4 + k][:, 0:P], ACT.Copy)
                    act.activation(PT[0:NS, 1, P * k:P * k + P], PS[4 + k][0:NS, P:2 * P], ACT.Copy)\
                        .then_inc(pt_copied, 1)

            act.wait_ge(pv_ready, UNITS)
            for j in range(2):
                attend_pair(0, j)
                act.wait_ge(pv_ready, UNITS + 2 * j + 2)
                for k in range(2):
                    load_cache(4 + 2 * j + k)
            for j in range(2):
                attend_pair(1, j)

            def gate(n, p, buf, tiles, sem=None, value=None):
                high(plus(n, 2))
                if sem is not None:
                    act.wait_ge(sem, value)
                halves(TMP[buf], p, ACT.Sigmoid).then_inc(slot_used[p.par], 1)
                for k in range(1, tiles):
                    high(plus(n, 2 + k))

            act.wait_ge(stored, 16 * (6 + 2 * SB))
            p1 = Idx(P_ATT + 1)
            for k in range(2):
                gate(Idx(N_ATT + 2 * k), Idx(P_ATT + 2 * k), k, 2)
            with act.Fori(1, KD // 2) as i:
                for k in range(2):
                    gate(Idx(N_ATT + 2 * k, i, 4), Idx(P_ATT + 2 * k, i, 4), k, 2,
                         slot_used[p1.par], i * 2 + (k + p1.half - 1))
            act.wait_ge(slot_used[p1.par], p1.half + KD)

            def z_tile(g, k, first=False):
                n = Idx(N_Z + k, g, 2)
                high(plus(n, 2))
                if not first:
                    act.wait_ge(yz_ready, g * 2 + (k - 1))
                halves(TMP[k], n, ACT.Silu).then_inc(slot_used[n.par], 1)

            def z_square(g, k, first=False):
                act.wait_ge(yz_ready, g * 2 + (k + 1))
                if not first:
                    act.wait_ge(zsq_used, g * 2 + (k - 1))
                act.activation(SQZ[k][:, :], at(UX, g * 2 + k), ACT.Square).then_inc(zsq_ready, 1)

            def z_std(g, first=False):
                act.wait_ge(zsq_used, g * 2 + 2)
                if not first:
                    act.wait_ge(yn_done, g)
                for h in range(2):
                    ins = act.activation(RINV[:, h * HT:(h + 1) * HT], PS[4 + h][:, 0:HT], ACT.Sqrt,
                                         bias=Q[:, Q_EPS:Q_EPS + 1], scale=float(NG) / INNER)
                ins.then_inc(zstd, 1)

            for k in range(2):
                z_tile(0, k, first=True)
            for k in range(2):
                z_square(0, k, first=True)
            for k in range(2):
                z_tile(1, k)
            z_std(0, first=True)
            for k in range(2):
                z_square(1, k)
            with act.Fori(2, NG) as g:
                for k in range(2):
                    z_tile(g, k)
                z_std(g - 1)
                for k in range(2):
                    z_square(g, k)
            z_std(NG - 1)

            for k in range(2):
                gate(Idx(N_SSM + 3 * k), Idx(P_SSM + 2 * k), k, 3)
            with act.Fori(1, KD // 2) as i:
                for k in range(2):
                    gate(Idx(N_SSM + 3 * k, i, 6), Idx(P_SSM + 2 * k, i, 4), k, 3, merged, i * 2 + (k - 1))
            act.wait_ge(yn_done, NG)
            act.dma_start(X[:, :, :], xT.rearrange("p (k t) -> p k t", k=KD)).then_inc(x_again, 16)
            norm(1, X, lambda k: (high(Idx(N_OUT + 2 + k)),
                                  act.wait_ge(slot_used[Idx(P_OUT + k).par], Idx(P_OUT + k).half + 1)))

            def queries(n, h, k, first=False):
                high(plus(n, 2))
                if not first:
                    act.wait_ge(score_ready, h - 1)
                halves(QP[k], plus(n, -P_SHIFT), ACT.Copy).then_inc(slot_used[n.par], 1)

            def early(n, k, turn, first=False):
                p = plus(n, -P_SHIFT)
                high(plus(n, 2))
                if not first:
                    act.wait_ge(act_out[k], turn * 16)
                halves(TMP[k], p, ACT.Gelu).then_inc(slot_used[p.par], 1)
                act.wait_ge(slot_used[p.par], p.half + 1)
                act.dma_start(dram(act_dram, turn)[:, k * T:(k + 1) * T], TMP[k][:, :]).then_inc(act_out[k], 16)

            def take_scores(h, k, first=False):
                act.wait_ge(score_ready, h + 1)
                if not first:
                    act.wait_ge(head_done, h - 1)
                for j in range(2):
                    act.activation(SCO[k][:, 0:CHUNKS, j, :],
                                   PS[4 + j][:, :].rearrange("p (c n) -> p c n", c=CHUNKS), ACT.Copy)
                    ins = act.activation(SCO[k][0:NS, CHUNKS, j, :], PS[6 + j][0:NS, 0:P], ACT.Copy)
                ins.then_inc(score_copied, 1)

            act.wait_ge(h_ready, 2 * KD)
            for k in range(2):
                queries(Idx(N_PQ + k), k, k, first=True)
            take_scores(0, 0, first=True)
            for k in range(2):
                early(Idx(N_PQ + 2 + k), k, 0, first=True)
            take_scores(1, 1, first=True)
            queries(Idx(N_PQ + 4), 2, 0)
            with act.Fori(0, 2) as i:
                for j in range(2):
                    n = Idx(N_PQ + 5 + 3 * j, i, 6)
                    for k in range(2):
                        early(plus(n, k), k, i * 2 + (1 + j))
                    take_scores(i * 2 + (2 + j), j)
                    queries(plus(n, 2), i * 2 + (3 + j), 1 - j)
            for j in range(2):
                n = Idx(N_PQ + 17 + 3 * j)
                for k in range(2):
                    early(plus(n, k), k, 5 + j)
                take_scores(6 + j, j)
                if j == 0:
                    queries(plus(n, 2), 7, 1)
            for k in range(2):
                early(Idx(N_ROUTE - 2 + k), k, PH - 1)

            def gate_exp(c):
                t0, L = chunk(c)
                for k in range(ROUTE_U):
                    if k == ROUTE_U // 2:
                        act.wait_ge(gmax, c + 1)
                        act.activation(EIJ[0:L, 2, :], EIJ[0:L, 2, :], ACT.Exp).then_inc(gexp, 1)
                    early(Idx(N_ROUTE + k, c, ROUTE_U), k % 2, c * (ROUTE_U // 2) + (PH + k // 2))

            gate_exp(0)
            with act.Fori(1, CHUNKS) as c:
                gate_exp(c)
            gate_exp(CHUNKS)

            def g_block(blk, buf, first=False):
                if not first:
                    act.wait_ge(g_out[buf], blk * 8 - buf * 8)
                with act.Fori(0, TB // 32) as j:
                    for t in range(2):
                        for k in range(QUADS):
                            act.wait_ge(g_ready, blk * (TB // 4) + j * 8 + (4 * t + k + 1))
                            out = GB[buf][:, :, bass.ds(j * 32 + (16 * t + 4 * k), 4)].rearrange("p i t -> p t i")
                            act.activation(out, PS[4 + k][:, :].rearrange("p (t i) -> p t i", t=4), ACT.Copy)\
                                .then_inc(g_copied, 1)
                        turn = blk * 2 + j
                        early(Idx(N_GU + t, turn, 2), t, turn + (EARLY - TURNS - STORE_U) // 2)
                act.wait_ge(g_copied, blk * (TB // 4) + TB // 4)
                act.dma_start(dram3(g_dram, blk), GB[buf][:, :, :]).then_inc(g_out[buf], 16)

            for b in range(2):
                g_block(b, b, first=True)
            with act.Fori(1, 4) as i:
                for b in range(2):
                    g_block(i * 2 + b, b)
            g_block(8, 0)
            for k in range(STORE_U):
                early(Idx(N_GU + TURNS + k), k % 2, EP + (k - STORE_U) // 2)
            act.wait_ge(g_out[0], 16 * 5)
            act.wait_ge(g_out[1], 16 * 4)
            for k in range(2):
                act.wait_ge(act_out[k], 16 * EP)

            def load_g(it, buf):
                act.dma_start(G2[buf][:, :, :, :], g_dram[:, :, bass.ds(it * 2, 2), :]).then_inc(g_in[buf], 16)

            def load_act(it, buf):
                act.dma_start(GE[buf][:, :, :].rearrange("p k t -> p (k t)"), dram(act_dram, it))\
                    .then_inc(act_in[buf], 16)

            def highs(n):
                for k in range(2):
                    high(plus(n, k), lag=4)

            for k in range(2):
                load_g(k, k)
                load_act(k, k)
            for k in range(2):
                high(Idx(N_LATE + 2 + k), lag=0)

            def late(it, i, j, stored_act=True):
                act.wait_ge(act_ready, it * 2 + 2)
                load_g(it + 2, j)
                if stored_act:
                    load_act(it + 2, j)
                highs(Idx(N_LATE + 4 + 2 * j, i, 4))

            with act.Fori(0, EP // 2 - 1) as i:
                for j in range(2):
                    late(i * 2 + j, i, j)
            late(EP - 2, EP // 2 - 1, 0, stored_act=False)

            def mixed(it, i, j, load=True, more=True):
                n, p = Idx(N_MIX + 4 * j, i, 8), Idx(P_LATE + 2 * j, i, 4)
                act.wait_ge(act_ready, it * 2 + 2)
                if load:
                    load_g(it + 2, 1 - j)
                for k in range(2):
                    high(plus(n, 4 + k), lag=4)
                    q = plus(p, k)
                    halves(GE[j][:, k, :], q, ACT.Gelu).then_inc(slot_used[q.par], 1)
                if more:
                    highs(plus(n, 6))

            turns = (ET // 2 - EP) // 2
            with act.Fori(0, turns - 1) as i:
                for j in range(2):
                    mixed(i * 2 + (EP - 1 + j), i, j)
            mixed(ET // 2 - 3, turns - 1, 0)
            mixed(ET // 2 - 2, turns - 1, 1, load=False, more=False)
            act.wait_ge(y_done, 1)
            norm(2, X)
            for k in range(KD):
                act.wait_ge(y_done, k + 2)
                act.dma_start(yT[:, k * T:(k + 1) * T], ACC[:, k, :]).then_inc(stored, 16)
            act.wait_ge(stored, 16 * (6 + 2 * SB + KD))

        @block.vector
        def _(dve):
            own = Chain(dve, dve_own)

            def halves(p, dst, src, op):
                for h in range(2):
                    cut = slice(h * HT, (h + 1) * HT)
                    ins = dve.tensor_tensor(dst[:, cut], PS[2 * p.par + h][:, 0:HT], src[:, cut], op)
                    if h == 0:
                        own.mark(ins)
                return ins

            def split(hi, lo, src):
                own.link(dve.tensor_copy(hi, src))
                return dve.tensor_tensor(lo, src, hi.bitcast(F32), ALU.subtract)

            def norm_h(turn, src, w0):
                dve.wait_ge(std_ready, turn + 1)
                own.link(dve.reciprocal(RINV[:, :], TMP[0][:, :]))
                for k in range(KD):
                    own.link(dve.scalar_tensor_tensor(TMP[k % 2][:, :], src[:, k, :], Q[:, w0 + k:w0 + k + 1],
                                                      RINV[:, :], ALU.mult, ALU.mult))
                    split(HH[:, k, :], HL[:, k, :], TMP[k % 2][:, :]).then_inc(h_ready, 1)

            dve.memset(ONES[:, :], 1.0).then_inc(setup, 1)
            dve.wait_ge(small_in, 48)
            dve.wait_ge(x_in, 16)
            norm_h(0, X, Q_MIX)

            V, E_, R_, W_, S_ = [t[0:NH, :] for t in (DV, DE, DR, DW, DP)]
            dve.wait_ge(slot_used[0], 1)
            dve.scalar_tensor_tensor(E_, V, -1.0, V, ALU.mult, ALU.max).then_inc(dt_abs, 1)
            for k in range(2):
                own.mark(dve.memset(PB[k][:, 0:3], 0.0))
            dve.wait_ge(dt_exp, 1)
            own.link(dve.tensor_scalar(S_, R_, 2.0, None, ALU.add))
            own.link(dve.reciprocal(W_, S_))
            own.link(dve.tensor_tensor(W_, W_, R_, ALU.mult))
            own.link(dve.tensor_tensor(E_, W_, W_, ALU.mult))
            own.link(dve.tensor_scalar(S_, E_, 1.0 / 15, None, ALU.mult))
            for odd in (13, 11, 9, 7, 5, 3):
                own.link(dve.scalar_tensor_tensor(S_, S_, 1.0 / odd, E_, ALU.add, ALU.mult))
            own.link(dve.scalar_tensor_tensor(S_, S_, 1.0, W_, ALU.add, ALU.mult))
            own.link(dve.tensor_scalar(V, V, 0.0, None, ALU.max))
            own.link(dve.scalar_tensor_tensor(S_, S_, 2.0, V, ALU.mult, ALU.add))
            dve.tensor_scalar(R_, S_, NA[0:NH, 0:1], -1.0, ALU.mult, ALU.mult).then_inc(dt_ready, 1)

            def conv(i, k, first=False):
                m = i * 2 + k
                n = Idx(N_XBC + k, i, 2)
                dve.wait_ge(slot_used[n.par], n.half + 1)
                if not first:
                    dve.wait_ge(silu_done, m - 1)
                    dve.nop(nofuse=True)
                out_p = CO[k][:, 0:SEQ]
                out_s = CO[k][:, SEQ:T].rearrange("p (b j) -> p b j", b=SB)

                def w(tap):
                    return Q[:, bass.ds(m * 4 + (Q_CW + tap), 1)]

                own.mark(dve.tensor_copy(SBF[k][:, :, 0:3], CIN[:, m] if isinstance(m, int) else
                                         CIN[:, bass.ds(m, 1), :, :].rearrange("p a b j -> p (a b) j")))
                own.mark(dve.tensor_scalar(out_p, PB[k][:, 0:SEQ], w(0), Q[:, bass.ds(m + Q_CB, 1)],
                                           ALU.mult, ALU.add))
                own.wait()
                own.mark(dve.tensor_scalar(out_s, SBF[k][:, :, 0:SL], w(0), Q[:, bass.ds(m + Q_CB, 1)],
                                           ALU.mult, ALU.add))
                for tap in range(1, 4):
                    own.mark(dve.scalar_tensor_tensor(out_p, PB[k][:, tap:tap + SEQ], w(tap), out_p,
                                                      ALU.mult, ALU.add))
                    own.wait()
                    if tap == 3:
                        own.mark(dve.tensor_copy(at(COP, m), PB[k][:, SEQ:SEQ + 3]))
                        dst = COS_[:, m] if isinstance(m, int) else \
                            COS_[:, bass.ds(m, 1), :, :].rearrange("p a b j -> p (a b) j")
                        own.mark(dve.tensor_copy(dst, SBF[k][:, :, SL:SL + 3]))
                    ins = dve.scalar_tensor_tensor(out_s, SBF[k][:, :, tap:tap + SL], w(tap), out_s,
                                                   ALU.mult, ALU.add)
                    if tap < 3:
                        own.mark(ins)
                ins.then_inc(conv_done, 1)

            for k in range(2):
                conv(0, k, first=True)
            with dve.Fori(1, CX // 2) as i:
                own.enter(i, 1, 20)
                for k in range(2):
                    conv(i, k)
                own.leave(CX // 2 - 1)

            dve.wait_ge(dtt_ready, 1)
            for half, dst in ((0, DTK), (NC, DAK)):
                a = PS[6][:, half * NH:(half + CHUNKS) * NH].rearrange("p (c h) -> p c h", h=NH)
                own.mark(dve.tensor_copy(dst[:, 0:CHUNKS, :], a))
                own.mark(dve.tensor_copy(dst[0:NS, CHUNKS, :],
                                         PS[6][0:NS, (half + CHUNKS) * NH:(half + NC) * NH]))
            dve.wait_ge(conv_done, CX)
            dve.wait_ge(silu_done, CX)
            own.link(dve.memset(S[:, :], 0.0))

            def ssd(c):
                t0, L = chunk(c)
                sample = isinstance(c, int) and c == CHUNKS
                start = isinstance(c, int) and c == 0
                mask = btri[0:L, 0:L] if sample else tri
                u0 = c * NG
                if not start:
                    dve.wait_ge(y_ready, u0)
                    dve.wait_ge(cs_ready, u0)
                own.mark(dve.tensor_copy(STX[:, :, 0:L], UX[:, :, bass.ds(t0, L)]))
                own.mark(dve.tensor_copy(STB[:, :, 0:L], UB[:, 0:NG, bass.ds(t0, L)]))
                if sample:
                    own.mark(dve.tensor_tensor(DAM[0:L, :, :], bc(bmask[0:L, :], NH),
                                               DAK[0:L, CHUNKS, :].unsqueeze(1).to_broadcast([L, SB, NH]),
                                               ALU.mult))
                own.mark(dve.tensor_copy(DTC[0:L, :], at(DTK, c)[0:L, :]))
                dve.tensor_copy(DAC[0:L, :], at(DAK, c)[0:L, :]).then_inc(staged, 1)
                dve.wait_ge(acum_ready, c + 1)
                own.link(dve.tensor_copy(AC[0:L, :], PS[2][0:L, 0:NH]))
                dve.tensor_tensor(DIF[0:L, :], PS[3][0:L, 0:NH], AC[0:L, :], ALU.subtract).then_inc(diff_ready, 1)
                dve.wait_ge(dexp_ready, c + 1)
                own.link(dve.tensor_tensor(DTE[0:L, :], DTE[0:L, :], DTC[0:L, :], ALU.mult))
                for q in range(4):
                    dve.wait_ge(turned, c * 6 + q + 1)
                    x = PS[6 + q % 2][0:L, :].rearrange("p (h d) -> p h d", d=HP)
                    for dst, w in ((XDT, DTC), (XDD, DTE)):
                        ins = dve.tensor_tensor(
                            dst[0:L, q * 512:(q + 1) * 512].rearrange("p (h d) -> p h d", d=HP), x,
                            bc(w[0:L, q * 8:(q + 1) * 8], HP), ALU.mult)
                        if w is DTC:
                            own.mark(ins)
                    ins.then_inc(turned_used, 1)
                for q in (4, 5):
                    dve.wait_ge(turned, c * 6 + q + 1)
                    dve.tensor_copy(BTK[0:L, 4 * (q - 4):4 * (q - 3), :],
                                    PS[6 + q % 2][0:L, :].rearrange("p (g n) -> p g n", g=4))\
                        .then_inc(turned_used, 1)

                def front(g):
                    u = u0 + g
                    if sample:
                        if g == 0:
                            dve.wait_ge(turned_used, c * 6 + 6)
                        if g >= 2:
                            dve.wait_ge(cs_ready, NG * CHUNKS + 4 * (g - 1))
                        dve.tensor_tensor(BMS[g % 2][0:L, :, :],
                                          BTK[0:L, g, :].unsqueeze(1).to_broadcast([L, SB, P]),
                                          bc(bmask[0:L, :], P), ALU.mult).then_inc(bms_ready, 1)
                    dve.wait_ge(acb_ready, u + 1)
                    dve.tensor_tensor(CBM[g % 2][0:L, 0:L], PS[2 + g % 2][0:L, 0:L], mask, ALU.mult)\
                        .then_inc(cb_ready, 1)

                def mid(g):
                    u = u0 + g
                    dve.wait_ge(e_ready, u + 1)
                    dve.wait_ge(cb_ready, u + 1)
                    own.mark(dve.tensor_tensor(
                        SEG[g % 2][0:L, :, 0:L], SEG[g % 2][0:L, :, 0:L],
                        CBM[g % 2][0:L, 0:L].unsqueeze(1).to_broadcast([L, 4, L]), ALU.mult))
                    dve.wait_ge(ec_ready, u + 1)
                    src = UB[:, NG + g, bass.ds(t0, L)].unsqueeze(1).to_broadcast([P, 4, L])
                    dve.tensor_tensor(CE[g % 2][:, :, 0:L], CE[g % 2][:, :, 0:L], src, ALU.mult)\
                        .then_inc(mt_ready, 1)

                def back(g):
                    u = u0 + g
                    dve.wait_ge(y_ready, u + 1)
                    for j in range(2):
                        m = 2 * g + j
                        y = UX[:, m, bass.ds(t0, L)]
                        ins = dve.scalar_tensor_tensor(y, y, Q[:, Q_DS + m:Q_DS + m + 1],
                                                       PS[4 + g % 2][:, j * P:j * P + L], ALU.mult, ALU.add)
                        if j == 0:
                            own.mark(ins)
                    ins.then_inc(y_used, 1)
                    if not sample:
                        dve.wait_ge(cs_ready, u + 1)
                        if not start:
                            dve.wait_ge(cs_used, u - NG + 1)
                        sg = S[:, 4 * g * HP:4 * (g + 1) * HP]
                        own.link(dve.tensor_tensor(sg.rearrange("p (r d) -> p r d", r=4),
                                                   sg.rearrange("p (r d) -> p r d", r=4),
                                                   bc(CD[:, 4 * g:4 * g + 4], HP), ALU.mult))
                        dve.tensor_tensor(sg, sg, PS[6 + g % 2][:, 0:4 * HP], ALU.add).then_inc(cs_used, 1)
                        return
                    for w in range(2):
                        h, v = 4 * g + 2 * w, 2 * g + w
                        s4 = S0[v % 3][:, :, :].rearrange("p b (r d) -> p b r d", r=2)
                        dve.wait_ge(s0_in[v % 3], 16 * (v // 3 + 1))
                        own.link(dve.tensor_tensor(s4, s4, bc(CDB[:, :, h:h + 2], HP), ALU.mult))
                        for half in range(2):
                            q = 4 * g + 2 * w + half
                            dve.wait_ge(cs_ready, NG * CHUNKS + q + 1)
                            part = S0[v % 3][:, 4 * half:4 * half + 4, :]
                            dve.tensor_tensor(part, part,
                                              PS[6 + half][:, :].rearrange("p (b c) -> p b c", b=4),
                                              ALU.add).then_inc(cs_used, 1)

                front(0)
                mid(0)
                for g in range(NG):
                    if g < NG - 1:
                        front(g + 1)
                        mid(g + 1)
                    back(g)

            ssd(0)
            with dve.Fori(1, CHUNKS) as c:
                own.enter(c, 1, 33)
                ssd(c)
                own.leave(CHUNKS - 1)
            ssd(CHUNKS)

            def rope(n, m, k, dst, first=False):
                dve.wait_ge(rs_ready, m + 1)
                halves(n, RT[k], CS[:, 0, :], ALU.mult).then_inc(slot_used[n.par], 1)
                own.mark(dve.tensor_tensor(RS[k][:, :], RS[k][:, :], CS[:, 1, :], ALU.mult))
                own.wait()
                dve.wait_ge(slot_used[n.par], n.half + 1)
                dve.tensor_tensor(dst, RT[k][:, :], RS[k][:, :], ALU.add).then_inc(rope_done, 1)

            dve.wait_ge(rope_in, 16)
            for k in range(2):
                rope(Idx(N_QKV + k), k, k, QT[:, k, :])
            with dve.Fori(1, 4) as i:
                own.enter(i, 1, 4)
                for k in range(2):
                    rope(Idx(N_QKV + k, i, 2), i * 2 + k, k, at(QT, i * 2 + k))
                own.leave(3)
            for k in range(2):
                rope(Idx(N_QKV + 8 + k), 8 + k, k, KP[:, k, WIN:WIN + T])
            own.mark(dve.memset(KP[:, :, 0:WIN], 0.0))
            own.mark(dve.memset(VK[:, 0, :], 0.0))
            dve.wait_ge(v_turned, 1)
            for c in range(NC):
                t0, L = chunk(c)
                lo = (c % 2) * 2 * P
                own.mark(dve.tensor_copy(VK[0:L, c + 1, :], PS[4 + c // 2][0:L, lo:lo + 2 * P]))
            own.mark(dve.tensor_copy(TMP[0][:, 0:2 * P], PS[7][:, 0:2 * P]))
            dve.tensor_copy(TMP[0][0:NS, 2 * P:4 * P], PS[7][0:NS, 2 * P:4 * P]).then_inc(v_tok, 1)
            own.wait()
            dve.wait_ge(v_tok, 1)
            dve.wait_ge(rope_done, 10)
            dve.wait_ge(mask_in, 32)

            def front(u):
                n, g = divmod(u, AKV)
                A = AM4[g % 2]
                dve.wait_ge(sc_ready, u + 1)
                if u >= 2:
                    dve.wait_ge(pt_ready, u - 1)
                mask = AM[:, min(n, 1), :].unsqueeze(1).to_broadcast([P, 2, 2 * WIN])
                for b in range(2):
                    ins = dve.tensor_tensor(SC[g % 2][:, 2 * b:2 * b + 2, :],
                                            PS[2 * (g % 2) + b][:, :].rearrange("p (r k) -> p r k", r=2),
                                            mask, ALU.add)
                    if b == 0:
                        own.mark(ins)
                ins.then_inc(sc_used, 1)
                own.wait()
                dve.wait_ge(sc_used, u + 1)
                own.link(dve.tensor_reduce(A[:, 0, :], SC[g % 2][:, :, :], AX.X, ALU.max))
                sink = Q[:, Q_SINK + 4 * g:Q_SINK + 4 * g + 4]
                own.link(dve.scalar_tensor_tensor(A[:, 1, :], A[:, 0, :], DH ** -0.5, sink,
                                                  ALU.mult, ALU.max))
                own.mark(dve.tensor_scalar(A[:, 2, :], A[:, 1, :], -1.0, None, ALU.mult))
                dve.tensor_tensor(A[:, 3, :], sink, A[:, 1, :], ALU.subtract).then_inc(m_ready, 1)

            def back(u):
                A = AM4[u % 2]
                dve.wait_ge(p_exp, u + 1)
                own.link(dve.tensor_tensor(A[:, 4, :], A[:, 4, :], A[:, 5, :], ALU.add))
                own.link(dve.reciprocal(A[:, 5, :], A[:, 4, :]))
                dve.tensor_tensor(SC[u % 2][:, :, :], SC[u % 2][:, :, :], bc(A[:, 5, :], 2 * WIN),
                                  ALU.mult).then_inc(p_ready, 1)

            def take(u):
                n, pr = u // AKV, u % AKV // 2
                dve.wait_ge(pv_ready, u + 1)
                o = PS[6 + pr][:, :].rearrange("p (r q) -> p r q", r=4)
                hi = OH[:, 4 * pr:4 * pr + 4, n * P:(n + 1) * P]
                own.link(dve.tensor_copy(hi, o))
                dve.tensor_tensor(OL[:, 4 * pr:4 * pr + 4, n * P:(n + 1) * P], o, hi.bitcast(F32),
                                  ALU.subtract).then_inc(o_done, 1)

            for u in range(2):
                front(u)
            back(0)
            for u in range(UNITS):
                if u < UNITS - 1:
                    back(u + 1)
                if u >= 2 and u % 2 == 0:
                    take(u - 1)
                if u < UNITS - 2:
                    front(u + 2)
            take(UNITS - 1)

            def attend_pair(i, j):
                bs = [i * 4 + (2 * j + k) for k in range(2)]
                cuts = [bass.ds(b * SL + SEQ, SL) for b in bs]
                sink = Q[:, Q_SSINK:Q_SSINK + 1]
                for k in range(2):
                    dve.tensor_copy(QS[:, k, :].rearrange("p (m j) -> p m j", m=KD), QT[:, :, cuts[k]])\
                        .then_inc(blk_staged, 1)
                for k in range(2):
                    b, u, A = bs[k], bs[k] + UNITS, AM4[k]
                    dve.wait_ge(sc_ready, u + 1)
                    dve.wait_ge(pt_ready, u - 1)
                    dve.tensor_tensor(SCS[k][:, :], PS[2 * k][:, 0:WIN + NS], at(SM, b), ALU.add)\
                        .then_inc(sc_used, 1)
                    dve.wait_ge(sc_used, u + 1)
                    own.link(dve.tensor_reduce(A[:, 0, 0:1], SCS[k][:, :], AX.X, ALU.max))
                    own.link(dve.scalar_tensor_tensor(A[:, 1, 0:1], A[:, 0, 0:1], DH ** -0.5, sink,
                                                      ALU.mult, ALU.max))
                    own.mark(dve.tensor_scalar(A[:, 2, 0:1], A[:, 1, 0:1], -1.0, None, ALU.mult))
                    dve.tensor_tensor(A[:, 3, 0:1], sink, A[:, 1, 0:1], ALU.subtract).then_inc(m_ready, 1)
                for k in range(2):
                    A = AM4[k]
                    dve.wait_ge(p_exp, bs[k] + (UNITS + 1))
                    own.link(dve.tensor_tensor(A[:, 4, 0:1], A[:, 4, 0:1], A[:, 5, 0:1], ALU.add))
                    own.link(dve.reciprocal(A[:, 5, 0:1], A[:, 4, 0:1]))
                    dve.tensor_scalar(SCS[k][:, :], SCS[k][:, :], A[:, 5, 0:1], None, ALU.mult)\
                        .then_inc(p_ready, 1)
                for k in range(2):
                    dve.wait_ge(pv_ready, bs[k] + (UNITS + 1))
                    o = PS[6 + k][:, 0:KD * SL].rearrange("p (m j) -> p m j", m=KD)
                    own.link(dve.tensor_copy(OH[:, :, cuts[k]], o))
                    dve.tensor_tensor(OL[:, :, cuts[k]], o, OH[:, :, cuts[k]].bitcast(F32), ALU.subtract)\
                        .then_inc(o_done, 1)

            with dve.Fori(0, SB // 4) as i:
                own.enter(i, 0, 24)
                for j in range(2):
                    attend_pair(i, j)
                own.leave(SB // 4)

            def att(n, p, g, m, buf):
                dve.wait_ge(tile_done, n.v + 1)
                dve.wait_ge(slot_used[g.par], g.half + 1)
                halves(p, at(ATT, m), TMP[buf], ALU.mult).then_inc(slot_used[p.par], 1)

            dve.wait_ge(o_done, 16)
            with dve.Fori(0, KD // 2) as i:
                own.enter(i, 0, 2)
                for k in range(2):
                    att(Idx(N_ATT + 2 * k + 1, i, 4), Idx(P_ATT + 2 * k + 1, i, 4),
                        Idx(P_ATT + 2 * k, i, 4), i * 2 + k, k)
                own.leave(KD // 2)

            def yz(g, k):
                n = Idx(N_Z + k, g, 2)
                dve.wait_ge(slot_used[n.par], n.half + 1)
                x = at(UX, g * 2 + k)
                dve.tensor_tensor(x, x, TMP[k][:, :], ALU.mult).then_inc(yz_ready, 1)

            def yn(g):
                dve.wait_ge(zstd, g + 1)
                dve.wait_ge(yz_ready, g * 2 + 2)
                own.link(dve.reciprocal(RINV[:, :], RINV[:, :]))
                for k in range(2):
                    m = g * 2 + k
                    own.mark(dve.scalar_tensor_tensor(ZT[k][:, :], at(UX, m), Q[:, bass.ds(m + Q_SNW, 1)],
                                                      RINV[:, :], ALU.mult, ALU.mult))
                own.wait()
                for k in range(2):
                    m = g * 2 + k
                    own.link(dve.tensor_copy(at(YH, m), ZT[k][:, :]))
                    ins = dve.tensor_tensor(at(YL, m), ZT[k][:, :], at(YH, m).bitcast(F32), ALU.subtract)
                    if k == 0:
                        own.mark(ins)
                ins.then_inc(yn_done, 1)

            for k in range(2):
                yz(0, k)
            with dve.Fori(1, NG) as g:
                own.enter(g, 1, 6)
                for k in range(2):
                    yz(g, k)
                yn(g - 1)
                own.leave(NG - 1)
            yn(NG - 1)

            def merge(i, k):
                n, p, g = Idx(N_SSM + 3 * k + 2, i, 6), Idx(P_SSM + 2 * k + 1, i, 4), Idx(P_SSM + 2 * k, i, 4)
                m = i * 2 + k
                dve.wait_ge(tile_done, n.v + 1)
                dve.wait_ge(slot_used[g.par], g.half + 1)
                halves(p, TMP[k], TMP[k], ALU.mult).then_inc(slot_used[p.par], 1)
                own.wait()
                dve.wait_ge(slot_used[p.par], p.half + 1)
                own.link(dve.tensor_tensor(TMP[k][:, :], TMP[k][:, :], at(ATT, m), ALU.add))
                dve.nop(nofuse=True)
                split(at(MH, m), at(ML, m), TMP[k][:, :]).then_inc(merged, 1)

            with dve.Fori(0, KD // 2) as i:
                own.enter(i, 0, 6)
                for k in range(2):
                    merge(i, k)
                own.leave(KD // 2)

            def residual(i, k):
                n, p = Idx(N_OUT + k, i, 2), Idx(P_OUT + k, i, 2)
                dve.wait_ge(tile_done, n.v + 1)
                x = at(X, i * 2 + k)
                halves(p, x, x, ALU.add).then_inc(slot_used[p.par], 1)

            dve.wait_ge(x_again, 16)
            with dve.Fori(0, KD // 2) as i:
                own.enter(i, 0, 2)
                for k in range(2):
                    residual(i, k)
                own.leave(KD // 2)
            own.wait()
            for k in range(2):
                p = Idx(P_OUT + KD - 2 + k)
                dve.wait_ge(slot_used[p.par], p.half + 1)
            norm_h(1, X, Q_FFN)

            def head(i, k):
                h = i * 2 + k
                dve.wait_ge(score_copied, h + 1)
                dve.nop(nofuse=True)
                for c in range(NC):
                    t0, L = chunk(c)
                    src = [SCO[k][0:L, c, j, :] for j in range(2)]
                    val = [TVH[0:L, c, j, :] for j in range(2)]
                    idx = [TIH[0:L, c, j, :] for j in range(2)]
                    rest = [SCR[j][0:L, :] for j in range(2)]
                    for j in range(2):
                        own.mark(dve.max(val[j][:, 0:8], src[j]))
                    own.wait(alone=True)
                    for j in range(2):
                        own.mark(dve.match_replace(rest[j], val[j][:, 0:8], src[j], -3.0e38))
                        own.mark(dve.max_index(idx[j][:, 0:8], val[j][:, 0:8], src[j]))
                    own.wait(alone=True)
                    for j in range(2):
                        own.mark(dve.max(val[j][:, 8:16], rest[j]))
                    own.wait(alone=True)
                    for j in range(2):
                        own.mark(dve.max_index(idx[j][:, 8:16], val[j][:, 8:16], rest[j]))
                own.wait(alone=True)
                for c0, c1, L in ((0, CHUNKS, P), (CHUNKS, NC, NS)):
                    for dst, src in ((TV, TVH), (TI, TIH)):
                        out = dst[0:L, c0:c1, bass.ds(h, 1), :, :].rearrange("p c a j k -> p c (a j k)")
                        ins = dve.tensor_copy(out, src[0:L, c0:c1, :, :].rearrange("p c j k -> p c (j k)"))
                        if L == P or dst is TV:
                            own.mark(ins)
                ins.then_inc(head_done, 1)
                own.wait()
                dve.wait_ge(head_done, h + 1)

            with dve.Fori(0, PH // 2) as i:
                own.enter(i, 0, 106)
                for k in range(2):
                    head(i, k)
                own.leave(PH // 2)
            own.wait(alone=True)
            dve.wait_ge(head_done, PH)

            def take_turned(c):
                t0, L = chunk(c)
                dve.wait_ge(parts_turned, c + 1)
                dve.tensor_copy(EJT[:, :, bass.ds(t0, L)],
                                PS[7][:, 0:3 * P].rearrange("p (s t) -> p s t", s=3)[:, :, 0:L])\
                    .then_inc(routed, 1)

            def route(c):
                t0, L = chunk(c)
                for dst, src in ((TVC, TV), (TIC, TI)):
                    s = src[0:L, c, :, :, :] if isinstance(c, int) else \
                        src[0:L, bass.ds(c, 1), :, :, :].rearrange("p a h j k -> p (a h) j k")
                    own.mark(dve.tensor_copy(dst[0:L, :, :, :], s))
                own.wait(alone=True)
                own.link(dve.tensor_tensor(
                    CMB[0:L, :, :, :], bc(TVC[0:L, :, 0, :], TOPK),
                    TVC[0:L, :, 1, :].unsqueeze(2).to_broadcast([L, PH, TOPK, TOPK]), ALU.add))
                dve.nop(nofuse=True)
                for h0 in range(0, PH, 2):
                    src = [CMB[0:L, h0 + j, :, :].rearrange("p a b -> p (a b)") for j in range(2)]
                    val = [BST[0:L, h0 + j, :] for j in range(2)]
                    idx = [PCK[0:L, h0 + j, :] for j in range(2)]
                    rest = [CMR[j][0:L, :] for j in range(2)]
                    for j in range(2):
                        own.mark(dve.max(val[j][:, 0:8], src[j]))
                    own.wait(alone=True)
                    for j in range(2):
                        own.mark(dve.match_replace(rest[j], val[j][:, 0:8], src[j], -3.0e38))
                        own.mark(dve.max_index(idx[j][:, 0:8], val[j][:, 0:8], src[j]))
                    own.wait(alone=True)
                    for j in range(2):
                        own.mark(dve.max(val[j][:, 8:16], rest[j]))
                    own.wait(alone=True)
                    for j in range(2):
                        own.mark(dve.max_index(idx[j][:, 8:16], val[j][:, 8:16], rest[j]))
                own.wait(alone=True)
                gates = EIJ[0:L, 2, :].rearrange("p (h k) -> p h k", h=PH)
                if not isinstance(c, int) or c > 0:
                    take_turned(c - 1)
                dve.tensor_tensor(gates, BST[0:L, :, :], BST[0:L, :, 0:1].to_broadcast([L, PH, TOPK]),
                                  ALU.subtract).then_inc(gmax, 1)
                pick = PCK[0:L, :, :].rearrange("p h k -> p (h k)")
                own.mark(dve.tensor_scalar(PAB[0:L, 0, :], pick, 4, None, ALU.logical_shift_right))
                own.link(dve.tensor_scalar(PAB[0:L, 1, :], pick, TOPK - 1, None, ALU.bitwise_and))
                own.link(dve.tensor_copy(PAF[0:L, :, :, :].rearrange("p s h k -> p (s h k)"),
                                         PAB[0:L, :, :].rearrange("p s k -> p (s k)")))
                steps = iota[0:L, 0:TOPK].unsqueeze(1).to_broadcast([L, PH * TOPK, TOPK])
                for s in range(2):
                    own.link(dve.tensor_tensor(
                        OHT[0:L, :, :, :].rearrange("p h k a -> p (h k) a"),
                        bc(PAF[0:L, s, :, :].rearrange("p h k -> p (h k)"), TOPK), steps, ALU.is_equal))
                    own.link(dve.tensor_tensor(
                        OHT[0:L, :, :, :], OHT[0:L, :, :, :],
                        TIC[0:L, :, s, :].unsqueeze(2).to_broadcast([L, PH, TOPK, TOPK]), ALU.mult))
                    own.link(dve.tensor_reduce(EIJ[0:L, s, :], OHT[0:L, :, :, :].rearrange(
                        "p h k a -> p (h k) a"), AX.X, ALU.add))
                dve.wait_ge(gexp, c + 1)
                own.link(dve.tensor_reduce(SUM[0:L, 0, :], gates, AX.X, ALU.add))
                own.link(dve.reciprocal(SUM[0:L, 1, :], SUM[0:L, 0, :]))
                dve.tensor_tensor(gates, gates, bc(SUM[0:L, 1, :], TOPK), ALU.mult).then_inc(parts_ready, 1)

            route(0)
            with dve.Fori(1, CHUNKS) as c:
                own.enter(c, 1, 54)
                route(c)
                own.leave(CHUNKS - 1)
            route(CHUNKS)
            take_turned(CHUNKS)
            dve.wait_ge(routed, NC)

            def one_hots(t, par, first=False):
                for k in range(QUADS):
                    buf = par * QUADS + k
                    if not first:
                        dve.wait_ge(g_ready, t * QUADS + (k + 1 - 2 * QUADS))
                    tok = bass.ds(t * (4 * QUADS) + 4 * k, 4)
                    own.mark(dve.tensor_tensor(OJ[buf][:, :, :], iota.unsqueeze(1).to_broadcast([P, 4, P]),
                                               bc(EJT[:, 1, tok], P), ALU.is_equal))
                    for q in range(4):
                        tok = bass.ds(t * (4 * QUADS) + (4 * k + q), 1)
                        ins = dve.tensor_scalar(AI[buf][:, q, :], iota, EJT[:, 0, tok], EJT[:, 2, tok],
                                                ALU.is_equal, ALU.mult)
                        if q < 3:
                            own.mark(ins)
                    ins.then_inc(hot_ready, 1)

            for j in range(2):
                one_hots(j, j, first=True)
            with dve.Fori(1, TURNS // 2) as i:
                own.enter(i, 1, 32)
                for j in range(2):
                    one_hots(i * 2 + j, j)
                own.leave(TURNS // 2 - 1)

            def acts(it, k, buf, p=None):
                dve.wait_ge(g_in[buf], (it - buf) * 8 + 16)
                if p is None:
                    dve.wait_ge(act_in[buf], (it - buf) * 8 + 16)
                else:
                    q = plus(p, k)
                    dve.wait_ge(slot_used[q.par], q.half + 1)
                ge = GE[buf][:, k, :].rearrange("p (b t) -> p b t", b=T // TB)
                own.link(dve.tensor_tensor(ge, ge, G2[buf][:, :, k, :], ALU.mult))
                split(ACH[buf][:, k, :], ACL[buf][:, k, :], GE[buf][:, k, :]).then_inc(act_ready, 1)

            def add_out(it, n, part):
                for q in range(part * KD, (part + 1) * KD):
                    d, h = q // 2, q % 2
                    if q < 2 * KD - 1:
                        dve.wait_ge(out_ready, it * 15 + (q + 1))
                    else:
                        dve.wait_ge(tile_done, n.v + 2)
                    a = ACC[:, d, h * HT:(h + 1) * HT]
                    if not isinstance(it, int) or it + q > 0:
                        dve.wait_ge(acc_done, it * 16 + q)
                    dve.tensor_tensor(a, a, PS[4 + q % 4][:, 0:HT], ALU.add).then_inc(acc_done, 1)

            def pair(it, n, buf, p=None):
                for part in range(2):
                    acts(it + 1, part, buf, p)
                    add_out(it, n, part)

            dve.wait_ge(g_out[0], 16 * 5)
            dve.wait_ge(g_out[1], 16 * 4)
            own.link(dve.memset(ACC[:, :, :], 0.0))
            for k in range(2):
                acts(0, k, 0)
            pair(0, Idx(N_LATE), 1)
            with dve.Fori(0, (EP - 2) // 2) as i:
                own.enter(i, 0, 8)
                for j in range(2):
                    pair(i * 2 + (1 + j), Idx(N_LATE + 2 + 2 * j, i, 4), j)
                own.leave((EP - 2) // 2)
            with dve.Fori(0, (ET // 2 - EP) // 2) as i:
                own.enter(i, 0, 8)
                for j in range(2):
                    pair(i * 2 + (EP - 1 + j), Idx(N_MIX + 4 * j + 2, i, 8), j, Idx(P_LATE + 2 * j, i, 4))
                own.leave((ET // 2 - EP) // 2)
            for part in range(2):
                add_out(ET // 2 - 1, Idx(N_ALL - 2), part)

            dve.wait_ge(acc_done, ET // 2 * 16)
            dve.tensor_tensor(X[:, :, :], X[:, :, :], ACC[:, :, :], ALU.add).then_inc(y_done, 1)
            dve.wait_ge(y_done, 1)
            dve.wait_ge(std_ready, 3)
            own.link(dve.reciprocal(RINV[:, :], TMP[0][:, :]))
            for k in range(KD):
                dve.scalar_tensor_tensor(ACC[:, k, :], X[:, k, :], Q[:, Q_FIN + k:Q_FIN + k + 1],
                                         RINV[:, :], ALU.mult, ALU.mult).then_inc(y_done, 1)



def kernel(x_prompt, x_sample, state_conv, state_ssm, cache_k_window, cache_v_window,
           norm_mix_w, w_in, conv_w, conv_b, dt_bias, a_log, d_skip, ssm_norm_w, w_ssm_out,
           attn_sinks, w_attn_out, w_out, norm_ffn_w, peer_w_q, peer_sub_keys, peer_u, peer_v,
           norm_final_w):
    import concourse.bacc as bacc
    from concourse.bass_utils import run_bass_kernel_spmd as run

    f = np.float32
    arr = {}
    tokens = np.concatenate([np.asarray(x_prompt)[0], np.asarray(x_sample).reshape(NS, D)], 0)
    arr["xT"] = tokens.T.reshape(KD, P, T).transpose(1, 0, 2).reshape(P, KD * T)

    win = np.asarray(w_in)[0]
    sizes = np.cumsum([0, INNER, CX * P, NH, AH_ * DH, AKV * DH, AKV * DH, D, D])
    o_z, o_x, o_dt, o_q, o_k, o_v, o_gs, o_ga = (int(v) for v in sizes[:8])

    def tile(w, c0):
        return w[:, c0:c0 + P].reshape(KD, P, P).transpose(1, 0, 2).reshape(1, P, D)

    def tiles(w, c0, n):
        return [tile(w, c0 + k * P) for k in range(n)]

    def pair_heads(w):
        return w.reshape(2, 2, 4, DH, -1).transpose(0, 2, 1, 3, 4).reshape(AH_ * DH, -1)

    wq = pair_heads(win[:, o_q:o_q + D].T).T
    wa = pair_heads(np.asarray(w_attn_out)[0])
    ws, wo, wpq = np.asarray(w_ssm_out)[0], np.asarray(w_out)[0], np.asarray(peer_w_q)[0]
    t = [tile(win, o_dt)] + tiles(win, o_x, CX) + tiles(wq, 0, KD) + tiles(win, o_k, 2) + tiles(win, o_v, 2)
    for m in range(KD):
        t += [tile(win, o_ga + m * P), tile(wa, m * P)]
    t += tiles(win, o_z, CI)
    for m in range(KD):
        t += [tile(win, o_gs + m * P), tile(ws[:D], m * P), tile(ws[D:], m * P)]
    t += tiles(wo, 0, KD)
    q = tiles(wpq, 0, PH)
    u = np.asarray(peer_u)[0].reshape(ET, P, KD, P).transpose(0, 3, 2, 1).reshape(ET, P, D)
    v = np.asarray(peer_v)[0].reshape(ET, P, D)
    t += q[0:2]
    for h in range(PH):
        t += [u[2 * h:2 * h + 2]] + q[h + 2:h + 3]
    t += [u[2 * PH:EARLY], v[0:2 * EP - 2]]
    for it in range(EP - 1, ET // 2 - 1):
        t += [u[2 * it + 2:2 * it + 4], v[2 * it:2 * it + 2]]
    t += [v[ET - 2:ET]]
    arr["wt"] = np.concatenate(t, 0)
    assert len(arr["wt"]) == N_ALL

    c = np.zeros((P, C_N), f)
    r = np.arange(P)
    c[:, C_ID:C_ID + P] = r[:, None] == r
    c[:, C_TRI:C_TRI + P] = r[:, None] <= r
    s, same = np.arange(NS), np.arange(NS)[:, None] // SL == np.arange(NS) // SL
    c[:NS, C_BTRI:C_BTRI + NS] = (s[:, None] <= s) & same
    c[:NS, C_BONE:C_BONE + NS] = same
    c[:NS, C_BM:C_BM + SB] = s[:, None] // SL == np.arange(SB)
    c[:, C_IOTA:C_IOTA + P] = r
    arr["consts"] = c
    half = DH // 2
    inv = np.power(f(10000.0), -(np.arange(half, dtype=f) / f(half))).astype(f)
    pos = np.concatenate([np.arange(SEQ), np.tile(2048 + np.arange(SL), SB)]).astype(f)
    ang = (pos[None, :] * inv[r % half][:, None]).astype(f)
    sign = np.where(r % DH < half, -1, 1)[:, None]
    arr["ropes"] = np.concatenate([np.cos(ang), np.sin(ang) * sign], 1).astype(f)
    q_, k_ = r[:, None], np.arange(2 * WIN)[None] - WIN
    band = (k_ <= q_) & (q_ - k_ < WIN)
    arr["amask"] = np.concatenate([np.where(band & (k_ >= 0), 0, NEG), np.where(band, 0, NEG)], 1).astype(f)
    j = (r % SL)[:, None]
    sm = [np.concatenate([np.where(r[None] > j, 0, NEG),
                          np.where((s[None] // SL == b) & (s[None] % SL <= j), 0, NEG)], 1) for b in range(SB)]
    arr["smask"] = np.concatenate(sm, 1).astype(f)

    def per_channel(v):
        return np.asarray(v).reshape(-1, P).T

    q = np.zeros((P, Q_N), f)
    q[:, Q_MIX:Q_MIX + KD] = per_channel(norm_mix_w[0])
    q[:, Q_FFN:Q_FFN + KD] = per_channel(norm_ffn_w[0])
    q[:, Q_FIN:Q_FIN + KD] = per_channel(norm_final_w)
    q[:, Q_CW:Q_CW + 4 * CX] = np.asarray(conv_w)[0].reshape(4, CX, P).transpose(2, 1, 0).reshape(P, 4 * CX)
    q[:, Q_CB:Q_CB + CX] = per_channel(conv_b[0])
    q[:, Q_SNW:Q_SNW + CI] = per_channel(ssm_norm_w[0])
    q[:, Q_DS:Q_DS + CI] = per_channel(np.repeat(np.asarray(d_skip)[0], HP))
    q[:, Q_SINK:Q_SINK + AH_] = np.asarray(attn_sinks)[0][None]
    q[:, Q_SSINK] = np.repeat(np.asarray(attn_sinks)[0], SL)
    q[:NH, Q_DTB] = np.asarray(dt_bias)[0]
    q[:NH, Q_AL] = np.asarray(a_log)[0]
    q[:, Q_EPS] = EPS
    arr["params"] = q
    arr["subk"] = np.asarray(peer_sub_keys)[0].transpose(0, 2, 1).reshape(P, P)
    arr["conv_in"] = np.asarray(state_conv)[0].reshape(SB, 3, CX, P).transpose(3, 2, 0, 1).reshape(P, CX * SB * 3)
    arr["s_in"] = np.asarray(state_ssm)[0].reshape(SB, NG, 2, 2 * HP, P).transpose(1, 2, 4, 0, 3)\
        .reshape(2 * NG, P, SB * P)
    ck, cv = np.asarray(cache_k_window)[0], np.asarray(cache_v_window)[0]
    arr["kct"] = ck.reshape(SB, WIN, 2, P).transpose(0, 3, 2, 1).reshape(SB, P, 2 * P)
    arr["kc"] = ck.reshape(SB, WIN, AKV * DH)
    arr["vc"] = cv.reshape(SB, WIN, AKV * DH)

    names = ["xT", "wt", "consts", "params", "subk", "conv_in", "ropes", "amask", "smask",
             "s_in", "kct", "kc", "vc"]
    outs = {"yT": (P, KD * T), "conv_p": (P, CX * 3), "conv_s": (P, CX * SB * 3), "ssm_p": (P, INNER),
            "ssm_s": (2 * NG, P, SB * P), "kw_p": (WIN, AKV * DH), "vw_p": (WIN, AKV * DH),
            "kw_s": (SB, WIN, AKV * DH), "vw_s": (SB, WIN, AKV * DH)}
    nc = bacc.Bacc("TRN2", target_bir_lowering=False, num_devices=1)
    args = []
    for n in names:
        arr[n] = np.ascontiguousarray(arr[n])
        args.append(nc.dram_tensor(n, arr[n].shape, F32, kind="ExternalInput").ap())
    for n, shape in outs.items():
        args.append(nc.dram_tensor(n, shape, F32, kind="ExternalOutput").ap())
    build(nc, *args)
    res = run(nc, [arr], core_ids=[0]).results[0]

    y = np.asarray(res["yT"]).reshape(P, KD, T).transpose(2, 1, 0).reshape(T, D)
    conv_p_ = np.asarray(res["conv_p"]).reshape(P, CX, 3).transpose(2, 1, 0).reshape(1, 1, 3, CX * P)
    conv_s_ = np.asarray(res["conv_s"]).reshape(P, CX, SB, 3).transpose(2, 3, 1, 0).reshape(1, SB, 3, CX * P)
    ssm_p_ = np.asarray(res["ssm_p"]).T.reshape(1, 1, NH, HP, P)
    ssm_s_ = np.asarray(res["ssm_s"]).reshape(NG, 2, P, SB, 2 * HP).transpose(3, 0, 1, 4, 2)\
        .reshape(1, SB, NH, HP, P)
    win_p = (1, 1, WIN, AKV, DH)
    win_s = (1, SB, WIN, AKV, DH)
    return (y[:SEQ].reshape(1, SEQ, D), y[SEQ:].reshape(SB, SL, D), conv_p_, ssm_p_,
            np.asarray(res["kw_p"]).reshape(win_p), np.asarray(res["vw_p"]).reshape(win_p),
            conv_s_, ssm_s_,
            np.asarray(res["kw_s"]).reshape(win_s), np.asarray(res["vw_s"]).reshape(win_s))
```
